# Optimizing a Trainium2 kernel written in Bass

```python
import jax, jax.numpy as jnp
from jax import lax
import numpy as np

D_MODEL = 1024
BATCH = 1
SEQ = 1024
DEPTH = 1
DEC_BATCH = 1
DEC_SEQ = 64
PAST_LEN = 2048

CHUNK = 64
RET_HEADS = 4
RET_DK = 128
RET_DV = 128
RET_WIDTH = RET_HEADS * RET_DV
SB_HEADS = 8
SB_HEAD_DIM = 64
SB_WIDTH = SB_HEADS * SB_HEAD_DIM
MIX_WIDTH = RET_WIDTH + SB_WIDTH
IN_WIDTH = 2 * RET_HEADS * RET_DK + 2 * RET_WIDTH + 3 * SB_WIDTH
SB_BLOCK = 128
ROPE_BASE = 10000.0
N_GROUPS = 4
EXPERTS_PER_GROUP = 4
N_EXPERTS = N_GROUPS * EXPERTS_PER_GROUP
TOP_K_IN_GROUP = 2
D_EXPERT = 512
DEEPNORM_ALPHA = (2.0 * DEPTH) ** 0.25
DEEPNORM_BETA = (8.0 * DEPTH) ** -0.25
LN_EPS = 1e-5

kernel_name = 'hymba_retention_stickbreaking_hmoe_stream_step'

def layer_norm_plain(x):
    xf = x.astype(jnp.float32)
    mu = jnp.mean(xf, axis=-1, keepdims=True)
    var = jnp.mean(jnp.square(xf - mu), axis=-1, keepdims=True)
    return (xf - mu) * lax.rsqrt(var + LN_EPS)

def layer_norm(x, g, b):
    return (layer_norm_plain(x) * g.astype(jnp.float32) + b.astype(jnp.float32)).astype(x.dtype)

def rms_norm_plain(x):
    xf = x.astype(jnp.float32)
    return xf * lax.rsqrt(jnp.mean(jnp.square(xf), axis=-1, keepdims=True) + LN_EPS)

def adaln_modulation(c, w, b):
    m = jnp.einsum('bd,de->be', jax.nn.silu(c), w) + b
    shift, scale, gate = jnp.split(m, 3, axis=-1)
    return shift[:, None, :], scale[:, None, :], gate[:, None, :]

def modulate(x, shift, scale):
    return (layer_norm_plain(x) * (1.0 + scale.astype(jnp.float32)) + shift.astype(jnp.float32)).astype(x.dtype)

def split_heads(t, n_heads):
    B, T, _ = t.shape
    return t.reshape(B, T, n_heads, -1).transpose(0, 2, 1, 3)

def merge_heads(t):
    B, H, T, d = t.shape
    return t.transpose(0, 2, 1, 3).reshape(B, T, H * d)

def rotary(x, pos):
    half = x.shape[-1] // 2
    inv = ROPE_BASE ** (-jnp.arange(half, dtype=jnp.float32) / half)
    ang = pos.astype(jnp.float32)[:, None] * inv[None, :]
    cos, sin = jnp.cos(ang), jnp.sin(ang)
    x1 = x[..., :half].astype(jnp.float32)
    x2 = x[..., half:].astype(jnp.float32)
    return jnp.concatenate([x1 * cos - x2 * sin, x2 * cos + x1 * sin], axis=-1).astype(x.dtype)

def retention(q, k, v, state0):
    B, H, T, dk = q.shape
    dv = v.shape[-1]
    C = min(CHUNK, T)
    N = T // C
    log_gamma = jnp.log1p(-jnp.exp2(-5.0 - jnp.arange(H, dtype=jnp.float32)))
    idx = jnp.arange(C, dtype=jnp.float32)
    rel = idx[:, None] - idx[None, :]
    decay = jnp.where(rel >= 0, jnp.exp(log_gamma[:, None, None] * jnp.maximum(rel, 0.0)), 0.0)
    q_decay = jnp.exp(log_gamma[:, None] * (idx + 1.0))[None, :, :, None]
    k_decay = jnp.exp(log_gamma[:, None] * (C - 1.0 - idx))[None, :, :, None]
    chunk_decay = jnp.exp(log_gamma * C)[None, :, None, None]
    qc = q.astype(jnp.float32).reshape(B, H, N, C, dk)
    kc = (k.astype(jnp.float32) * dk ** -0.5).reshape(B, H, N, C, dk)
    vc = v.astype(jnp.float32).reshape(B, H, N, C, dv)
    scores = jnp.einsum('bhncd,bhnmd->bhncm', qc, kc) * decay[None, :, None]
    intra = jnp.einsum('bhncm,bhnme->bhnce', scores, vc)

    def step(state, xs):
        qn, kn, vn = xs
        inter = jnp.einsum('bhcd,bhde->bhce', qn * q_decay, state)
        state = state * chunk_decay + jnp.einsum('bhcd,bhce->bhde', kn * k_decay, vn)
        return state, inter

    state, inter = lax.scan(step, state0.astype(jnp.float32),
                            (jnp.moveaxis(qc, 2, 0), jnp.moveaxis(kc, 2, 0), jnp.moveaxis(vc, 2, 0)))
    out = intra + jnp.moveaxis(inter, 0, 2)
    return out.reshape(B, H, T, dv), state

def stick_breaking(q, k, v, q_offset):
    B, H, Tq, d = q.shape
    Tk = k.shape[2]
    blk = min(SB_BLOCK, Tq)
    nb = Tq // blk
    qb = jnp.moveaxis(q.reshape(B, H, nb, blk, d), 2, 0)
    kpos = jnp.arange(Tk)

    def one_block(args):
        qi, i = args
        tpos = q_offset + i * blk + jnp.arange(blk)
        z = jnp.einsum('bhqd,bhkd->bhqk', qi, k).astype(jnp.float32) * (d ** -0.5)
        mask = (kpos[None, :] < tpos[:, None])[None, None]
        log_beta = jax.nn.log_sigmoid(z)
        log_one_minus = jnp.where(mask, jax.nn.log_sigmoid(-z), 0.0)
        later = lax.cumsum(log_one_minus, axis=3, reverse=True) - log_one_minus
        weights = jnp.where(mask, jnp.exp(log_beta + later), 0.0)
        return jnp.einsum('bhqk,bhkd->bhqd', weights.astype(v.dtype), v)

    out = lax.map(one_block, (qb, jnp.arange(nb)))
    return jnp.moveaxis(out, 0, 2).reshape(B, H, Tq, d)

def hybrid_mixer(h, pos0, ret_state0, k_past, v_past, w_in, ret_norm_g, sb_norm_g, w_out):
    T = h.shape[1]
    proj = jnp.einsum('btd,de->bte', h, w_in)
    sizes = (RET_HEADS * RET_DK, RET_HEADS * RET_DK, RET_WIDTH, RET_WIDTH, SB_WIDTH, SB_WIDTH, SB_WIDTH)
    rq, rk, rv, rg, sq, sk, sv = jnp.split(proj, np.cumsum(sizes)[:-1].tolist(), axis=-1)
    pos = pos0 + jnp.arange(T)
    ret_o, ret_state = retention(rotary(split_heads(rq, RET_HEADS), pos), rotary(split_heads(rk, RET_HEADS), pos),
                                 split_heads(rv, RET_HEADS), ret_state0)
    ret_o = merge_heads(layer_norm_plain(ret_o)) * ret_norm_g.astype(jnp.float32) * jax.nn.silu(rg.astype(jnp.float32))
    sq = split_heads(sq, SB_HEADS)
    sk = split_heads(sk, SB_HEADS)
    sv = split_heads(sv, SB_HEADS)
    if k_past is None:
        k_all, v_all = sk, sv
    else:
        k_all = jnp.concatenate([k_past.astype(sk.dtype), sk], axis=2)
        v_all = jnp.concatenate([v_past.astype(sv.dtype), sv], axis=2)
    sb_o = stick_breaking(sq, k_all, v_all, k_all.shape[2] - T)
    sb_o = merge_heads(rms_norm_plain(sb_o)) * sb_norm_g.astype(jnp.float32)
    mixed = jnp.concatenate([ret_o, sb_o], axis=-1).astype(h.dtype)
    return jnp.einsum('bte,ed->btd', mixed, w_out), sk, sv, ret_state

def hier_moe(h, w_group, b_group, w_router, b_router, w_e_gate, w_e_up, w_e_down):
    B, T, D = h.shape
    hf = h.reshape(B * T, D)
    g_logits = (hf @ w_group + b_group).astype(jnp.float32)
    g_prob = jax.nn.softmax(g_logits, axis=-1)
    g_idx = jnp.argmax(g_logits, axis=-1)
    g_p = jnp.take_along_axis(g_prob, g_idx[:, None], axis=-1)
    e_logits = (hf @ w_router + b_router).astype(jnp.float32).reshape(-1, N_GROUPS, EXPERTS_PER_GROUP)
    e_in = jnp.take_along_axis(e_logits, g_idx[:, None, None], axis=1)[:, 0]
    top_v, top_i = lax.top_k(e_in, TOP_K_IN_GROUP)
    top_w = jax.nn.softmax(top_v, axis=-1) * g_p
    expert_id = g_idx[:, None] * EXPERTS_PER_GROUP + top_i
    combine = jnp.sum(jax.nn.one_hot(expert_id, N_EXPERTS, dtype=jnp.float32) * top_w[..., None], axis=1)
    combine = combine.astype(h.dtype)
    y = jnp.zeros_like(hf)
    for e in range(N_EXPERTS):
        a = jax.nn.silu(hf @ w_e_gate[e]) * (hf @ w_e_up[e])
        y = y + combine[:, e:e + 1] * (a @ w_e_down[e])
    return y.reshape(B, T, D)

def trunk(x, c, pos0, ret_state0, past_k, past_v, weights):
    (w_in, w_out, ret_norm_g, sb_norm_g, w_ada_mix, b_ada_mix, ln_mix_g, ln_mix_b,
     w_ada_ffn, b_ada_ffn, ln_ffn_g, ln_ffn_b, w_group, b_group, w_router, b_router,
     w_e_gate, w_e_up, w_e_down) = weights
    new_k, new_v, new_r = [], [], []
    for l in range(DEPTH):
        shift, scale, gate = adaln_modulation(c, w_ada_mix[l], b_ada_mix[l])
        h = modulate(x, shift, scale)
        kp = None if past_k is None else past_k[l]
        vp = None if past_v is None else past_v[l]
        mix, k_l, v_l, r_l = hybrid_mixer(h, pos0, ret_state0[l], kp, vp, w_in[l], ret_norm_g[l], sb_norm_g[l], w_out[l])
        x = layer_norm(DEEPNORM_ALPHA * x + gate * mix, ln_mix_g[l], ln_mix_b[l])
        shift, scale, gate = adaln_modulation(c, w_ada_ffn[l], b_ada_ffn[l])
        h = modulate(x, shift, scale)
        ffn = hier_moe(h, w_group[l], b_group[l], w_router[l], b_router[l], w_e_gate[l], w_e_up[l], w_e_down[l])
        x = layer_norm(DEEPNORM_ALPHA * x + gate * ffn, ln_ffn_g[l], ln_ffn_b[l])
        new_k.append(k_l)
        new_v.append(v_l)
        new_r.append(r_l)
    return x, jnp.stack(new_k, 0), jnp.stack(new_v, 0), jnp.stack(new_r, 0)

def setup_inputs(seed: int = 0) -> dict:
    key = jax.random.key(seed)
    ks = jax.random.split(key, 32)

    def nrm(k, shape, scale):
        return jax.random.normal(k, shape, jnp.float32) * scale

    col_scale = jnp.concatenate([
        jnp.ones((2 * RET_HEADS * RET_DK,), jnp.float32),
        jnp.full((RET_WIDTH,), DEEPNORM_BETA, jnp.float32),
        jnp.ones((RET_WIDTH,), jnp.float32),
        jnp.ones((2 * SB_WIDTH,), jnp.float32),
        jnp.full((SB_WIDTH,), DEEPNORM_BETA, jnp.float32),
    ])
    return {
        'x_prompt': nrm(ks[0], (BATCH, SEQ, D_MODEL), 1.0),
        'x_sample': nrm(ks[1], (DEC_BATCH, DEC_SEQ, D_MODEL), 1.0),
        'cache_sb_k': nrm(ks[2], (DEPTH, DEC_BATCH, SB_HEADS, PAST_LEN, SB_HEAD_DIM), 1.0),
        'cache_sb_v': nrm(ks[3], (DEPTH, DEC_BATCH, SB_HEADS, PAST_LEN, SB_HEAD_DIM), DEEPNORM_BETA),
        'state_ret': nrm(ks[4], (DEPTH, DEC_BATCH, RET_HEADS, RET_DK, RET_DV), 1.0),
        'c_prompt': nrm(ks[5], (BATCH, D_MODEL), 1.0),
        'c_sample': nrm(ks[6], (DEC_BATCH, D_MODEL), 1.0),
        'w_in': nrm(ks[7], (DEPTH, D_MODEL, IN_WIDTH), D_MODEL ** -0.5) * col_scale,
        'w_out': nrm(ks[8], (DEPTH, MIX_WIDTH, D_MODEL), MIX_WIDTH ** -0.5 * DEEPNORM_BETA),
        'ret_norm_g': 1.0 + nrm(ks[9], (DEPTH, RET_WIDTH), 0.02),
        'sb_norm_g': 1.0 + nrm(ks[10], (DEPTH, SB_WIDTH), 0.02),
        'w_ada_mix': nrm(ks[11], (DEPTH, D_MODEL, 3 * D_MODEL), 0.5 * D_MODEL ** -0.5),
        'b_ada_mix': nrm(ks[12], (DEPTH, 3 * D_MODEL), 0.02),
        'ln_mix_g': 1.0 + nrm(ks[13], (DEPTH, D_MODEL), 0.02),
        'ln_mix_b': nrm(ks[14], (DEPTH, D_MODEL), 0.02),
        'w_ada_ffn': nrm(ks[15], (DEPTH, D_MODEL, 3 * D_MODEL), 0.5 * D_MODEL ** -0.5),
        'b_ada_ffn': nrm(ks[16], (DEPTH, 3 * D_MODEL), 0.02),
        'ln_ffn_g': 1.0 + nrm(ks[17], (DEPTH, D_MODEL), 0.02),
        'ln_ffn_b': nrm(ks[18], (DEPTH, D_MODEL), 0.02),
        'w_group': nrm(ks[19], (DEPTH, D_MODEL, N_GROUPS), D_MODEL ** -0.5),
        'b_group': nrm(ks[20], (DEPTH, N_GROUPS), 0.01),
        'w_router': nrm(ks[21], (DEPTH, D_MODEL, N_EXPERTS), D_MODEL ** -0.5),
        'b_router': nrm(ks[22], (DEPTH, N_EXPERTS), 0.01),
        'w_e_gate': nrm(ks[23], (DEPTH, N_EXPERTS, D_MODEL, D_EXPERT), D_MODEL ** -0.5),
        'w_e_up': nrm(ks[24], (DEPTH, N_EXPERTS, D_MODEL, D_EXPERT), D_MODEL ** -0.5),
        'w_e_down': nrm(ks[25], (DEPTH, N_EXPERTS, D_EXPERT, D_MODEL), D_EXPERT ** -0.5 * DEEPNORM_BETA),
    }

def reference(x_prompt, x_sample, cache_sb_k, cache_sb_v, state_ret, c_prompt, c_sample,
              w_in, w_out, ret_norm_g, sb_norm_g, w_ada_mix, b_ada_mix, ln_mix_g, ln_mix_b,
              w_ada_ffn, b_ada_ffn, ln_ffn_g, ln_ffn_b, w_group, b_group, w_router, b_router,
              w_e_gate, w_e_up, w_e_down):
    weights = (w_in, w_out, ret_norm_g, sb_norm_g, w_ada_mix, b_ada_mix, ln_mix_g, ln_mix_b,
               w_ada_ffn, b_ada_ffn, ln_ffn_g, ln_ffn_b, w_group, b_group, w_router, b_router,
               w_e_gate, w_e_up, w_e_down)
    ret_zero = jnp.zeros((DEPTH, x_prompt.shape[0], RET_HEADS, RET_DK, RET_DV), jnp.float32)
    y_prompt, sb_k_prompt, sb_v_prompt, ret_state_prompt = trunk(
        x_prompt, c_prompt, 0, ret_zero, None, None, weights)
    y_sample, sb_k_sample, sb_v_sample, ret_state_sample = trunk(
        x_sample, c_sample, cache_sb_k.shape[3], state_ret, cache_sb_k, cache_sb_v, weights)
    return (y_prompt, y_sample, sb_k_prompt, sb_v_prompt, ret_state_prompt, sb_k_sample, sb_v_sample, ret_state_sample)


_drawn_inputs = setup_inputs


def setup_inputs(seed=0):
    import zlib

    import numpy as np

    out = dict(_drawn_inputs(seed))
    spreads = {}
    factors = {'cache_sb_k': 8.0,
     'cache_sb_v': 3.83,
     'ret_norm_g': 54.286,
     'sb_norm_g': 35.362,
     'ln_mix_g': 7.223,
     'ln_mix_b': 7.629,
     'b_ada_ffn': 33.979,
     'ln_ffn_g': 8.027,
     'ln_ffn_b': 8.307,
     'b_group': 64.0,
     'b_router': 64.0,
     'w_ada_ffn': 2.801,
     'w_group': 2.933,
     'w_router': 3.405,
     'w_e_gate': 2.841}
    for name, (base, spread) in spreads.items():
        noise = np.random.default_rng([zlib.crc32(name.encode()), seed]).standard_normal(out[name].shape)
        drawn = base * np.exp(spread * noise) if base else spread * noise
        out[name] = __import__('jax').numpy.asarray(drawn.astype(out[name].dtype))
    for name, factor in factors.items():
        out[name] = (out[name] * factor).astype(out[name].dtype)
    return out
```

```python
from contextlib import ExitStack

import numpy as np

import concourse.bass as bass
from concourse import mybir

ALU = mybir.AluOpType
ACT = mybir.ActivationFunctionType
AX = mybir.AxisListType
F32 = mybir.dt.float32
BF16 = mybir.dt.bfloat16
I32 = mybir.dt.int32

P = 128
D = 1024
KC = D // P
SEQ = 1024
DEC = 64
PAST = 2048
TILES = SEQ // P + 1
LAST = TILES - 1
TOK = SEQ + DEC
RET_HEADS = 4
SB_HEADS = 8
PAIRS = SB_HEADS // 2
HD = 64
GROUPS = 4
EPG = 4
EXPERTS = 16
F = 512
FC = F // P
ALPHA = 2.0 ** 0.25
EPS = 1e-5
NEG = -1.0e30
CHUNK_SCALE = HD ** -0.5
MAX_BLOCKS = 33
LOG_GAMMA = np.log1p(-np.exp2(-5.0 - np.arange(RET_HEADS)))
STEPS_BEFORE = [0, 9, 18, 27, 39, 48, 57, 66]

C_IDENT = 0
C_CAUSAL = 128
C_NEG = C_CAUSAL + 128
C_NEGS = C_NEG + 128
C_GQ = C_NEGS + 64
C_GK = C_GQ + 4
C_TRI = C_GK + 4
C_FIRST = C_TRI + 128
C_VALID = C_FIRST + 4
C_LIMIT = C_VALID + TILES
C_MAIN = C_LIMIT + 8
C_COS = C_MAIN
C_SIN = C_COS + TILES * 64
C_END = C_SIN + TILES * 128


def shape_constants():
    c = np.zeros((P, C_END), np.float32)
    i = np.arange(P)
    c[:, C_IDENT:C_IDENT + 128] = np.eye(P)
    inv = np.float32(10000.0) ** (-np.arange(64, dtype=np.float32) / np.float32(64))
    for t in range(TILES):
        pos = (i + t * P if t < LAST else PAST + i).astype(np.float32)
        ang = (pos[:, None] * inv[None, :]).astype(np.float64)
        c[:, C_COS + 64 * t:C_COS + 64 * t + 64] = np.cos(ang)
        c[:, C_SIN + 128 * t:C_SIN + 128 * t + 64] = -np.sin(ang)
        c[:, C_SIN + 128 * t + 64:C_SIN + 128 * t + 128] = np.sin(ang)
    c[:, C_CAUSAL:C_CAUSAL + 128] = i[:, None] <= i[None, :]
    c[:, C_NEG:C_NEG + 128] = np.where(i[None, :] >= i[:, None], NEG, 0.0)
    c[:, C_NEGS:C_NEGS + 64] = np.where(i[None, :64] >= (i % 64)[:, None], NEG, 0.0)
    for h in range(RET_HEADS):
        c[:, C_GQ + h] = np.exp(LOG_GAMMA[h] * (i + 1))
        c[:, C_GK + h] = np.exp(-LOG_GAMMA[h] * (i + 1)) * 128.0 ** -0.5
    c[:, C_TRI:C_TRI + 128] = i[:, None] < i[None, :]
    c[:, C_FIRST:C_FIRST + 4] = [4, 3, 2, 1]
    c[:, C_VALID:C_VALID + TILES] = 1.0
    c[64:, C_VALID + LAST] = 0.0
    c[:, C_LIMIT:C_LIMIT + 8] = 128.0 * np.arange(1, 9)
    return c


class Steps:

    def __init__(self, eng, sem):
        self.eng, self.sem, self.n = eng, sem, 0

    def __call__(self, ins):
        ins.then_inc(self.sem, 1)
        self.n += 1
        self.eng.wait_ge(self.sem, self.n)


def rows_of(t):
    return P if t < LAST else DEC


def attention_units():
    units = []
    for pair in range(PAIRS):
        for a in range(2):
            for i in range(SEQ // P):
                hi = i + 1
                while hi > 0:
                    lo = max(0, hi - 4)
                    units.append((pair, a, i, list(range(lo, hi)), hi == i + 1, lo == 0))
                    hi = lo
        for lo, hi in ((13, 17), (9, 13), (5, 9), (1, 5), (0, 1)):
            units.append((pair, None, LAST, list(range(lo, hi)), hi == 17, lo == 0))
    return units


def stream_step(nc, a):
    (x_prompt, x_sample, cache_k, cache_v, state_ret, c_prompt, c_sample, w_in, w_out, ret_norm_g, sb_norm_g,
     w_ada_mix, b_ada_mix, ln_mix_g, ln_mix_b, w_ada_ffn, b_ada_ffn, ln_ffn_g, ln_ffn_b, w_group, b_group,
     w_router, b_router, w_e_gate, w_e_up, w_e_down, consts, y_prompt, y_sample, k_prompt, v_prompt,
     state_prompt, k_sample, v_sample, state_sample, mod_rows, x1_dram, h2_dram, y_dram) = a

    with ExitStack() as ctx:
        arena = ctx.enter_context(nc.sbuf_tensor("arena", [P, 53100], F32))
        psum = [ctx.enter_context(nc.psum_tensor(f"psum{i}", [P, 2, 512], F32)) for i in range(4)]

        def bank(i):
            return psum[i // 2][:, i % 2, :]

        def sem(name):
            return ctx.enter_context(nc.semaphore(name))

        top = [0]

        def region(n):
            off = top[0]
            top[0] += n
            return off

        def view(off, *dims, dt=F32):
            n = int(np.prod(dims))
            v = arena[:, off:off + n]
            if dt is not F32:
                v = v.bitcast(dt)
            names = "abcd"[:len(dims)]
            if len(dims) == 1:
                return v
            return v.rearrange(f"p ({' '.join(names)}) -> p {' '.join(names)}",
                               **{k: d for k, d in zip(names, dims)})

        r_const = region(C_MAIN)
        r_small = region(1550)
        r_tmp = region(2560)
        r_a = region(8704)
        r_w = region(8192)
        r_m = region(9216)
        r_sq = region(4352)
        r_b = region(17920)
        assert top[0] <= 53100, top[0]

        cst = view(r_const, C_MAIN)
        rot = view(r_sq, C_END - C_MAIN)
        ident = cst[:, C_IDENT:C_IDENT + 128]

        small = [r_small]

        def tiny(*dims, dt=F32):
            off = small[0]
            small[0] += int(np.prod(dims))
            assert small[0] <= r_small + 1550
            return view(off, *dims, dt=dt)

        half_ident = tiny(64).bitcast(BF16)
        half_neg = tiny(64).bitcast(BF16)
        half_negs = tiny(32).bitcast(BF16)
        half_tri = tiny(64).bitcast(BF16)
        half_ones = tiny(64).bitcast(BF16)
        mhalf = tiny(36)
        colv = tiny(72)
        csig = tiny(16)
        silu_c = tiny(8, 2)
        modv = tiny(2, 16)
        rows = tiny(128)
        ones_col = tiny(1)
        stats = tiny(2, 6)
        mv = tiny(9, 2)
        ve = tiny(36)
        rstd = tiny(36)
        nmr = tiny(36)
        rstd_b = tiny(36)
        ln_ve = tiny(18)
        ln_rstd = tiny(18)
        ln_nmr = tiny(18)
        ln_mv = tiny(18, 2)
        sb_sq = tiny(9, 8)
        sb_rstd = tiny(9, 8)
        ret_stats = tiny(36, 6)
        ret_m = tiny(36)
        ret_d = tiny(36)
        router_w = tiny(8, 20)
        router_b = tiny(20)
        tok_i = tiny(9, dt=I32)

        xt = view(r_m, 9, D)
        mixed = view(r_m, 9, D)
        hT = view(r_a, KC, TOK)
        mixT = view(r_a, KC, TOK)
        ada_b = [view(r_b + 4096 * i, KC, 512) for i in range(4)]
        ada_m = [view(r_m + 4096 * i, KC, 512) for i in range(2)]
        ada_rows = view(r_sq + C_END - C_MAIN, 2048)
        bias_row = view(r_sq + C_END - C_MAIN, 2, 512)
        row_out = view(r_sq + C_END - C_MAIN + 1024, 2, 512)
        ada_acc = view(r_m + 8192, 2, 512)
        win = [view(r_w + 4096 * i, KC, 512) for i in range(2)]
        wout = view(r_w, KC, D)

        qhT = view(r_b, 4, TOK)
        khT = view(r_b + 4352, 4, TOK)
        kh = view(r_b + 8704, 9, 4, 128)
        vr = view(r_b + 13312, 9, 4, 128)
        sqT = view(r_sq, 4, TOK)
        skT = view(r_b, 4, TOK)
        sv = view(r_b + 4352, 9, 512)
        rope_a = view(r_tmp, 4, 128)
        rope_b = view(r_tmp + 512, 4, 128)
        rope_c = view(r_tmp + 1024, 4, 128)
        nat = [view(r_tmp + 1536 + 512 * i, 4, 128) for i in range(2)]
        U = view(r_tmp, 2, 4, 128)
        state_in = view(r_tmp + 1024, 4, 128)
        state_out = view(r_tmp + 1536, 4, 128)
        masked = view(r_tmp + 2048, 2, 128)
        kvs = view(r_tmp + 2304, 2, 128)
        gate_sig = view(r_tmp, 2, 512)
        gate_lin = view(r_tmp + 1024, 2, 512)

        s_rot, s_const, s_rows, s_router = sem("rotations_in"), sem("const_in"), sem("rows_in"), sem("router_in")
        s_xb = [sem(f"x_in{i}") for i in range(3)]
        s_adaB = [sem(f"ada_first_in{i}") for i in range(4)]
        s_adaM = [sem(f"ada_later_in{i}") for i in range(2)]
        s_win = [sem(f"win_in{i}") for i in range(2)]
        s_wout, s_state = sem("wout_in"), sem("state_in")
        s_dv, s_ac, s_po = sem("dve_steps"), sem("act_steps"), sem("pool_steps")
        s_rowT, s_colv, s_csig, s_silu = [sem(n) for n in
            ("rows_turned", "columns_ready", "c_sigmoid", "silu_ready")]
        s_ve, s_rstd, s_xn = sem("variance_ready"), sem("rstd_ready"), sem("x_normed")
        s_adap, s_adae, s_adat, s_mod = [sem(n) for n in
            ("first_ada_ready", "first_ada_copied", "first_ada_turned", "modulation_ready")]
        s_bias = [sem(f"bias_row_in{i}") for i in range(2)]
        s_acc, s_rsum, s_rowo = sem("ada_products"), sem("ada_summed"), sem("mod_row_ready")
        s_modw = [sem(f"mod_row_out{i}") for i in range(2)]
        s_sq = sem("sb_squares")
        s_lt, s_leA, s_leD = sem("x_turned"), sem("hT_by_act"), sem("hT_by_dve")
        s_proj, s_freeA, s_freeD = sem("projected"), sem("projection_read_act"), sem("projection_read_dve")
        s_ra, s_rc, s_rope = sem("rope_parts"), sem("rope_sum"), sem("rope_done")
        s_tr, s_tre = sem("projection_turned"), sem("turned_copied")
        s_ko, s_vo, s_so = [sem(f"k_out{i}") for i in range(2)], sem("v_out"), sem("state_out")
        s_sc, s_kv, s_ro = sem("ret_scores"), sem("ret_kv"), sem("ret_out")
        s_sm, s_kvs, s_U, s_oev = sem("scores_masked"), sem("kv_scaled"), sem("state_updated"), sem("ret_out_copied")
        s_rve, s_rrs, s_gs, s_gm, s_mr = [sem(n) for n in
            ("ret_variance", "ret_rstd", "gate_sigmoid", "gate_ready", "ret_mixed")]
        s_kc = [sem(f"cache_k_in"), sem("cache_v_in")]
        s_qk, s_sig, s_scan, s_wm, s_wt = [sem(n) for n in
            ("scores_ready", "sigmoids_ready", "scan_done", "weights_ready", "weights_turned")]
        s_wte, s_pv, s_ov = [sem(n) for n in
            ("turned_weights_copied", "values_summed", "sb_out_copied")]
        s_kt, s_kte, s_ones = sem("cache_k_turned"), sem("cache_k_copied"), sem("scan_start_ones")
        s_sbv, s_sbr, s_sbn = sem("sb_variance"), sem("sb_rstd"), sem("sb_normed")
        s_mt, s_meA, s_meD = sem("mixed_turned"), sem("mixT_by_act"), sem("mixT_by_dve")
        s_brow, s_x5 = sem("row_tables_in"), [sem(f"x_again_in{i}") for i in range(2)]
        s_op, s_ope, s_ve1, s_nm1, s_ve2, s_nm2 = [sem(n) for n in
            ("out_projected", "out_read", "ln_variance", "ln_shift", "ln0_variance", "ln0_shift")]
        s_xh, s_x1, s_h2a, s_h2 = sem("ln_applied"), sem("x1_ready"), sem("h_scaled"), sem("h2_ready")
        s_x1o, s_h2o = [sem(f"x1_out{i}") for i in range(2)], [sem(f"h2_out{i}") for i in range(2)]
        s_ht, s_hte, s_lg = sem("h2_turned"), sem("h2T_copied"), sem("logits_ready")
        s_rt1, s_rt2, s_asg, s_rank, s_route = [sem(n) for n in
            ("exp_inputs", "exps_ready", "assigned", "ranks_ready", "routed")]
        s_iota, s_oh, s_ids, s_gi = [sem(n) for n in
            ("counts_ready", "one_hots_ready", "lists_summed", "lists_ready")]
        s_e = [[sem(f"expert_{w}_in{i}") for w in ("gate", "up", "down")] for i in range(2)]
        s_edone = sem("expert_done")
        s_idx, s_hg, s_htr, s_hT = sem("index_ready"), sem("rows_gathered"), sem("rows_turned2"), sem("block_hT")
        s_gu, s_sg, s_g1, s_aT, s_yp, s_ye, s_ys = [sem(n) for n in
            ("gate_up_ready", "gate_sig", "gate_silu", "act_ready", "down_ready", "y_copied", "y_stored")]
        s_frow = sem("final_rows_in")
        s_y0 = [sem(f"y_gathered{t}") for t in range(TILES)]
        s_x1i = sem("x1_in")
        s_cve, s_crs, s_cnm, s_cxh, s_cg, s_cy = [sem(n) for n in
            ("fin_variance", "fin_first", "fin_shift", "fin_applied", "fin_gained", "fin_ready")]
        s_cacc, s_yo = sem("fin_sum"), sem("y_out")
        s_go = sem("queue_order")
        s_fill = sem("unused_rows_cleared")

        units = attention_units()
        NU = len(units)
        per_pair = NU // PAIRS
        outs_before = []
        n = 0
        for u in units:
            outs_before.append(n)
            n += u[5]
        N_OUT = n
        ov_after = []
        for u in units:
            if u[5]:
                ov_after.append((ov_after[-1] if ov_after else 0) + (1 if u[2] < LAST else 2))

        col_of = [0, 512, 1024, 2048, 1536, 2560, 3072]
        reader = ["D", "D", "A", "A", "D", "A", "A"]
        steps = []
        for g in range(7):
            if g == 3:
                steps += [(g, pr, ch) for pr in range(4) for ch in range(3)]
            else:
                steps += [(g, t, 0) for t in range(TILES)]
        NS = len(steps)
        assert NS == STEPS_BEFORE[7]
        free_count = []
        cnt = {"A": 0, "D": 0}
        for g, _, _ in steps:
            cnt[reader[g]] += 1
            free_count.append((reader[g], cnt[reader[g]]))
        events = []
        ada_at = {1 + int(1.5 * i): i for i in range(16)}
        turn_no = 0
        lag = []
        ret_i = 0
        for k, (g, t, ch) in enumerate(steps):
            if k == STEPS_BEFORE[4]:
                for i in range(ret_i, 36 + 1):
                    events.append(("ret", i))
                ret_i = 37
                events.append(("retfin",))
            events.append(("proj", k))
            if g in (0, 1, 5):
                lag.append((k, g, t))
            while lag and (k - lag[0][0] >= 2):
                _, g2, t2 = lag.pop(0)
                events.append(("turn", turn_no, g2, t2))
                turn_no += 1
            for name, later in (("adaout", 2), ("adasum", 1), ("ada", 0)):
                if k - later in ada_at:
                    events.append((name, ada_at[k - later]))
            if g == 3 and k > STEPS_BEFORE[3]:
                for _ in range(3):
                    if ret_i <= 36:
                        events.append(("ret", ret_i))
                        ret_i += 1
        N_TURN = turn_no
        assert N_TURN == 27

        def ada_src(j):
            w = w_ada_mix if j < 6 else w_ada_ffn
            return w[0, :, (j % 6) * 512:(j % 6 + 1) * 512].rearrange("(k p) n -> p k n", p=P)

        def ret_pos(i):
            return i // 4, i % 4

        def gamma_chunk(t, h):
            return float(np.exp(LOG_GAMMA[h] * rows_of(t)))

        r_at = r_b + 8960
        om = view(r_at, 3, 512)
        be = view(r_at + 1536, 3, 512)
        wgt = view(r_at + 3072, 3, 512)
        wT = view(r_at + 4608, 3, 4, 128)
        pf = view(r_at + 6144, 3, 514)
        pc = view(r_at + 6144 + 1542, 2, 514)
        sq_junk = view(r_tmp, 64)
        kTs = view(r_a, PAST)
        kc = view(r_a + 2048, 16, 2, 64)
        vc = view(r_a + 4096, 16, 2, 64)
        first_no, cont_no = [], []
        nf = ncn = 0
        for u in units:
            first_no.append(nf)
            cont_no.append(ncn)
            if u[4]:
                nf += 1
            else:
                ncn += 1

        def width(u):
            _, a_, i, tl, _, _ = units[u]
            return sum(64 if (i == LAST and t == 16) else 128 for t in tl)

        def scan_buf(u):
            if units[u][4]:
                return pf[:, first_no[u] % 3, :]
            return pc[:, cont_no[u] % 2, :]

        rows5 = view(r_b, 8, D)
        xin = view(r_b + 8192, 2, D)
        t1 = view(r_b + 8192 + 2048, 2, D)
        x1 = view(r_b + 8192 + 4096, 2, D)
        h2 = view(r_b + 8192 + 6144, 2, D)
        h2T = view(r_b + 8192 + 8192, KC, P)

        ew = [[view(r_m, KC, F), view(r_m + 4096, KC, F), view(r_sq, FC, D)],
              [view(r_a, KC, F), view(r_a + 4096, KC, F), view(r_w, FC, D)]]
        rows8 = view(r_b, 4, D)
        hg = view(r_b + 4096, D)
        hTb = view(r_b + 5120, KC, P)
        aT = view(r_b + 6144, FC, P)
        sgb = view(r_b + 6656, 2, P)
        g1b = view(r_b + 6912, 2, P)
        yb = view(r_b + 7168, D)
        ya = [view(r_m + D * t, D) for t in range(TILES)]
        yc = [view(r_a + D * t if t < LAST else r_sq, D) for t in range(TILES)]
        x1c = [view(r_b + 8192 + D * t if t < 6 else r_w + 4096 + D * (t - 6), D) for t in range(TILES)]
        zero_rows = view(r_b + 16384, D)

        rt = [r_tmp]

        def rtiny(*dims, dt=F32):
            off = rt[0]
            rt[0] += int(np.prod(dims))
            assert rt[0] <= r_tmp + 2560
            return view(off, *dims, dt=dt)

        lg = rtiny(9, 20)
        gmax = rtiny(9)
        eq = rtiny(9, 4)
        eqm = rtiny(9)
        oh = rtiny(9, 4)
        gsub = rtiny(9, 4)
        gsum = rtiny(9)
        gp = rtiny(9)
        prod = rtiny(9, 16)
        ein = rtiny(9, 4)
        v0 = rtiny(9)
        v1 = rtiny(9)
        a0 = rtiny(9, 4)
        a1 = rtiny(9, 4)
        dd = rtiny(9)
        w0 = rtiny(9)
        w1 = rtiny(9)
        A0 = rtiny(9, 16)
        A1 = rtiny(9, 16)
        Ab = rtiny(72).bitcast(BF16)
        tot = rtiny(9, 16)
        prior = rtiny(9, 16)
        cnt16 = rtiny(16)
        cmp8 = rtiny(16, 8)
        nb = rtiny(16)
        incl = rtiny(16)
        table_f = rtiny(17)
        table = rtiny(17, dt=I32)
        slots = rtiny(9, 16)
        sk_f = rtiny(2, 9)
        slot_i = rtiny(2, 9, dt=I32)
        gi = rtiny(MAX_BLOCKS, dt=I32)
        tok_f = rtiny(9)
        place_oh = view(r_b, 18, P)
        past = view(r_b + 2304, 18, MAX_BLOCKS + 1)
        block_oh = view(r_b + 3072, 18, MAX_BLOCKS)
        block_tok = view(r_b + 3840, 18, MAX_BLOCKS)
        starts = view(r_b + 4608, MAX_BLOCKS + 1)
        places = view(r_b + 4672, P)
        starts_i = view(r_b + 4864, MAX_BLOCKS + 1, dt=I32)
        places_i = view(r_b + 4928, P, dt=I32)
        slot_block = view(r_b + 5120, 18)
        slot_place = view(r_b + 5184, 18)
        idc = rtiny(1, dt=I32)

        def weights_turned(act, u):
            _, _, i, tl, _, _ = units[u]
            b = bank(3 + u % 2).rearrange("p (t q) -> p t q", q=P)
            act.wait_ge(s_wt, u + 1)
            if u >= 3:
                act.wait_ge(s_pv, u - 2)
            n_full = len(tl) - (i == LAST and tl[-1] == 16)
            last = nc.scalar.activation(wT[:, u % 3, 0:n_full], b[:, 0:n_full], ACT.Copy)
            if n_full < len(tl):
                last = nc.scalar.activation(wT[0:64, u % 3, n_full], b[0:64, n_full], ACT.Copy)
            last.then_inc(s_wte, 1)

        def norm_scalars(step, G, r, col):
            c = slice(col, col + 1)
            step(G.tensor_tensor(ln_rstd[0:r, c], ln_ve[0:r, c], mhalf[0:r, 0:1], ALU.pow))
            step(G.tensor_tensor(ln_nmr[0:r, c], ln_mv[0:r, col, 0:1], ln_rstd[0:r, c], ALU.mult))
            return G.tensor_scalar(ln_nmr[0:r, c], ln_nmr[0:r, c], -1.0, None, ALU.mult)

        block = ctx.enter_context(nc.Block())

        @block.sync
        def _(sp):
            sp.dma_start(cst, consts[:, 0:C_MAIN]).then_inc(s_const, 16)
            for off, src, nr in ((0, c_prompt[0], 8), (8, c_sample[0], 8), (16, b_ada_mix[0], 24),
                                 (40, b_ada_ffn[0], 24), (64, ret_norm_g[0], 4), (68, sb_norm_g[0], 4)):
                sp.dma_start(rows[off:off + nr, :], src.rearrange("(r c) -> r c", r=nr)).then_inc(s_rows, 16)
            sp.dma_start(xt[:, 0:4, :], x_prompt[0, 0:512, :].rearrange("(t p) d -> p t d", p=P)).then_inc(s_xb[0], 16)
            for j in range(2):
                sp.dma_start(ada_b[j], ada_src(j)).then_inc(s_adaB[j], 16)
            sp.dma_start(xt[:, 4:8, :], x_prompt[0, 512:1024, :].rearrange("(t p) d -> p t d", p=P)).then_inc(s_xb[1], 16)
            sp.dma_start(xt[0:DEC, LAST, :], x_sample[0]).then_inc(s_xb[2], 16)
            for j in range(2, 4):
                sp.dma_start(ada_b[j], ada_src(j)).then_inc(s_adaB[j], 16)

            def load_win(g):
                if g >= 2:
                    sp.wait_ge(s_proj, STEPS_BEFORE[g - 1])
                sp.dma_start(win[g % 2], w_in[0, :, col_of[g]:col_of[g] + 512].rearrange("(k p) n -> p k n", p=P)
                             ).then_inc(s_win[g % 2], 16)

            def load_ada(j):
                if j < 6:
                    sp.wait_ge(s_lt, 24)
                    sp.wait_ge(s_adat, 4)
                else:
                    sp.wait_ge(s_acc, 2 * (j - 5))
                sp.dma_start(ada_m[j % 2], ada_src(j)).then_inc(s_adaM[j % 2], 16)
                if j >= 6:
                    sp.wait_ge(s_rowo, 2 * (j - 5))
                b = (b_ada_mix if j < 6 else b_ada_ffn)[0:1, (j % 6) * 512:(j % 6 + 1) * 512]
                sp.dma_start(bias_row[0:1, j % 2], b).then_inc(s_bias[j % 2], 16)

            load_win(0)
            sp.dma_start(rot, consts[:, C_MAIN:C_END]).then_inc(s_rot, 16)
            load_win(1)
            sp.dma_start(router_w[:, :, 0:4], w_group[0].rearrange("(k p) n -> p k n", p=P)).then_inc(s_router, 16)
            sp.dma_start(router_w[:, :, 4:20], w_router[0].rearrange("(k p) n -> p k n", p=P)).then_inc(s_router, 16)
            sp.dma_start(router_b[:, 0:4], b_group[0].unsqueeze(0).to_broadcast([P, 4])).then_inc(s_router, 16)
            sp.dma_start(router_b[:, 4:20], b_router[0].unsqueeze(0).to_broadcast([P, 16])).then_inc(s_router, 16)
            for j in (4, 5, 6, 7):
                load_ada(j)
            load_win(2)
            for j in (8, 9, 10, 11):
                load_ada(j)
            load_win(3)
            sp.wait_ge(s_tre, 18)
            sp.wait_ge(s_rope, 18)
            sp.dma_start(state_in, state_ret[0, 0].rearrange("h k v -> k h v")).then_inc(s_state, 16)
            load_win(4)
            sp.wait_ge(s_U, 36)
            sp.dma_start(state_prompt[0, 0].rearrange("h k v -> k h v"), U[:, 0]).then_inc(s_so, 16)
            sp.dma_start(state_sample[0, 0].rearrange("h k v -> k h v"), state_out).then_inc(s_so, 16)
            load_win(5)
            load_win(6)
            base_a = 21
            for t in range(TILES):
                r = rows_of(t)
                sp.wait_ge(s_freeA, base_a + t + 1)
                dst = k_prompt[0, 0, :, t * P:t * P + r, :] if t < LAST else k_sample[0, 0]
                sp.dma_start(dst.rearrange("h s d -> s h d"),
                             nat[t % 2][0:r].rearrange("p a b -> p (a b)").rearrange("p (h d) -> p h d", h=8)).then_inc(s_ko[t % 2], 16)
            for t in range(TILES):
                r = rows_of(t)
                sp.wait_ge(s_freeA, base_a + 9 + t + 1)
                dst = v_prompt[0, 0, :, t * P:t * P + r, :] if t < LAST else v_sample[0, 0]
                sp.dma_start(dst.rearrange("h s d -> s h d"),
                             sv[0:r, t, :].rearrange("p (h d) -> p h d", h=8)).then_inc(s_vo, 16)
            sp.wait_ge(s_proj, NS)

            def load_cache(pair):
                if pair:
                    sp.wait_ge(s_kt, 4 * pair)
                for hh in range(2):
                    sp.dma_start(kc[:, :, hh, :], cache_k[0, 0, 2 * pair + hh].rearrange("(t p) d -> p t d", p=P)
                                 ).then_inc(s_kc[0], 16)
                if pair:
                    sp.wait_ge(s_pv, per_pair * pair)
                for hh in range(2):
                    sp.dma_start(vc[:, :, hh, :], cache_v[0, 0, 2 * pair + hh].rearrange("(t p) d -> p t d", p=P)
                                 ).then_inc(s_kc[1], 16)

            load_cache(0)
            sp.dma_start(wout, w_out[0].rearrange("(k p) n -> p k n", p=P)).then_inc(s_wout, 16)
            for pair in range(1, PAIRS):
                load_cache(pair)
            sp.wait_ge(s_pv, NU)
            for i in range(2):
                sp.wait_ge(s_modw[i], 16 * 8)
            sp.wait_ge(s_vo, 16 * TILES)

            def mod_row(ada, s, part):
                return mod_rows[ada, s:s + 1, part * D:(part + 1) * D].to_broadcast([P, D])

            for slot, src in enumerate((mod_row(0, 0, 2), mod_row(0, 1, 2), mod_row(1, 0, 1), mod_row(1, 1, 1),
                                        mod_row(1, 0, 0), mod_row(1, 1, 0),
                                        ln_mix_g[0].unsqueeze(0).to_broadcast([P, D]),
                                        ln_mix_b[0].unsqueeze(0).to_broadcast([P, D]))):
                sp.dma_start(rows5[:, slot, :], src).then_inc(s_brow, 16)
            sp.wait_ge(s_ov, N_OUT + PAIRS)

            def load_x(t):
                r = rows_of(t)
                if t >= 2:
                    sp.wait_ge(s_ve1, t - 1)
                src = x_prompt[0, t * P:t * P + r, :] if t < LAST else x_sample[0]
                sp.dma_start(xin[0:r, t % 2, :], src).then_inc(s_x5[t % 2], 16)

            def store_5(t):
                r = rows_of(t)
                sp.wait_ge(s_x1, t + 1)
                sp.dma_start(x1_dram[t * P:t * P + r, :], x1[0:r, t % 2, :]).then_inc(s_x1o[t % 2], 16)
                sp.wait_ge(s_h2, t + 1)
                sp.dma_start(h2_dram[t * P:t * P + r, :], h2[0:r, t % 2, :]).then_inc(s_h2o[t % 2], 16)

            load_x(0)
            load_x(1)

            def load_expert(e, k):
                for i, w in enumerate((w_e_gate, w_e_up, w_e_down)):
                    sp.dma_start(ew[k][i], w[0, e].rearrange("(k p) n -> p k n", p=P)).then_inc(s_e[k][i], 16)

            sp.wait_ge(s_mt, 24)
            load_expert(0, 0)
            for t in range(TILES):
                if t + 2 < TILES:
                    load_x(t + 2)
                store_5(t)
            sp.wait_ge(s_op, TILES)
            load_expert(1, 1)
            sp.wait_ge(s_lg, 9)
            sp.wait_ge(s_x1o[0], 16 * 5)
            sp.wait_ge(s_h2o[0], 16 * 5)
            sp.wait_ge(s_x1o[1], 16 * 4)
            sp.wait_ge(s_h2o[1], 16 * 4)
            sp.wait_ge(s_h2, 9)
            sp.wait_ge(s_hg, 16)
            for slot, src in enumerate((mod_row(1, 0, 2), mod_row(1, 1, 2),
                                        ln_ffn_g[0].unsqueeze(0).to_broadcast([P, D]),
                                        ln_ffn_b[0].unsqueeze(0).to_broadcast([P, D]))):
                sp.dma_start(rows8[:, slot, :], src).then_inc(s_frow, 16)
            for t in range(TILES):
                r = rows_of(t)
                sp.dma_start(x1c[t][0:r], x1_dram[t * P:t * P + r, :]).then_inc(s_x1i, 16)
            sp.wait_ge(s_route, 1)
            total = sp.value_load(table[0:1, 16:17], min_val=1, max_val=MAX_BLOCKS - 1)
            with sp.Fori(total, MAX_BLOCKS) as b:
                sp.dma_start(y_dram[bass.ds(b * P, P), :], zero_rows).then_inc(s_fill, 16)
            with sp.Fori(1, EXPERTS // 2) as ee:
                for k in range(2):
                    sp.wait_ge(s_edone, 2 * ee + k - 1)
                    for i, w in enumerate((w_e_gate, w_e_up, w_e_down)):
                        src = w[0, bass.ds(2 * ee + k, 1)].rearrange("e (k p) n -> p (e k) n", p=P)
                        sp.dma_start(ew[k][i], src).then_inc(s_e[k][i], 16)

            for t in range(TILES):
                r = rows_of(t)
                sp.wait_ge(s_cy, t + 1)
                dst = y_prompt[0, t * P:t * P + r, :] if t < LAST else y_sample[0]
                sp.dma_start(dst, ya[t][0:r]).then_inc(s_yo, 16)
            sp.wait_ge(s_yo, 16 * TILES)
            sp.wait_ge(s_ko[0], 16 * 5)
            sp.wait_ge(s_ko[1], 16 * 4)
            sp.wait_ge(s_so, 32)

        @block.tensor
        def _(pe):
            pe_last = [None]

            def mm(*x, **y):
                pe_last[0] = nc.tensor.matmul(*x, **y)
                return pe_last[0]

            pe.wait_ge(s_const, 16)
            pe.wait_ge(s_rows, 96)
            nc.tensor.transpose(bank(7)[:, 0:72], rows[0:72, :], ident[0:72, 0:72]).then_inc(s_rowT, 1)

            pe.wait_ge(s_silu, 1)
            for j in range(5):
                if j < 4:
                    pe.wait_ge(s_adaB[j], 16)
                    if j >= 2:
                        pe.wait_ge(s_adae, j - 1)
                    for k in range(KC):
                        last = mm(bank(6 + j % 2)[0:2, :], silu_c[:, k, :], ada_b[j][:, k, :],
                                  start=(k == 0), stop=(k == KC - 1))
                    last.then_inc(s_adap, 1)
                if j >= 1:
                    pe.wait_ge(s_adae, j)
                    for e in range(4 * j - 4, 4 * j):
                        last = nc.tensor.transpose(bank(5)[:, 2 * e:2 * e + 2], ada_rows[0:2, e * P:(e + 1) * P],
                                                   ident[0:2, 0:2])
                    last.then_inc(s_adat, 1)
            n = 0
            for b, (t0, t1_) in enumerate(((0, 4), (4, 8), (8, 9))):
                pe.wait_ge(s_xn, t1_)
                for k in range(KC):
                    if n >= 4:
                        pe.wait_ge(s_leA if n % 2 == 0 else s_leD, (n - 4) // 2 + 1)
                    for t in range(t0, t1_):
                        r = rows_of(t)
                        c0 = (t - t0) * P
                        last = nc.tensor.transpose(bank(n % 4)[:, c0:c0 + r], xt[0:r, t, k * P:(k + 1) * P],
                                                   ident[0:r, 0:r])
                    last.then_inc(s_lt, 1)
                    n += 1

            def proj(k):
                g, t, ch = steps[k]
                if k == 0:
                    pe.wait_ge(s_leA, 12)
                    pe.wait_ge(s_leD, 12)
                if k == STEPS_BEFORE[g]:
                    pe.wait_ge(s_win[g % 2], 16 * (g // 2 + 1))
                if k >= 3:
                    e, c = free_count[k - 3]
                    pe.wait_ge(s_freeA if e == "A" else s_freeD, c)
                w = win[g % 2]
                for c in range(KC):
                    if g == 3:
                        c0, cw = ch * 512, (512 if ch < 2 else DEC)
                        last = mm(bank(k % 3)[:, 0:cw], w[:, c, t * P:(t + 1) * P], hT[:, c, c0:c0 + cw],
                                  start=(c == 0), stop=(c == KC - 1))
                    else:
                        r = rows_of(t)
                        last = mm(bank(k % 3)[0:r, :], hT[:, c, t * P:t * P + r], w[:, c, :],
                                  start=(c == 0), stop=(c == KC - 1))
                last.then_inc(s_proj, 1)

            def turn(n, g, t):
                r = rows_of(t)
                if n >= 2:
                    pe.wait_ge(s_tre, n - 1)
                if g < 2:
                    pe.wait_ge(s_rope, n + 1)
                    src = nat[n % 2] if g == 0 else kh[:, t]
                else:
                    pe.wait_ge(s_freeA, 21 + t + 1)
                    src = nat[t % 2]
                b = bank(3 if n % 2 == 0 else 7)
                for h in range(4):
                    last = nc.tensor.transpose(b[:, h * P:h * P + r], src[0:r, h, :], ident[0:r, 0:r])
                last.then_inc(s_tr, 1)

            def ret(i):
                if i < 36:
                    t, h = ret_pos(i)
                    r = rows_of(t)
                    if i == 0:
                        pe.wait_ge(s_tre, 18)
                        pe.wait_ge(s_rope, 18)
                        pe.wait_ge(s_freeA, 9)
                        pe.wait_ge(s_rowo, 16)
                    if i >= 1:
                        pe.wait_ge(s_sm, i)
                        pe.wait_ge(s_kvs, i)
                    mm(bank(4)[0:r, 0:r], khT[:, h, t * P:t * P + r], qhT[:, h, t * P:t * P + r],
                       start=True, stop=True).then_inc(s_sc, 1)
                    mm(bank(6)[:, 0:128], kh[0:r, t, h, :], vr[0:r, t, h, :], start=True, stop=True).then_inc(s_kv, 1)
                if i >= 1:
                    j = i - 1
                    t, h = ret_pos(j)
                    r = rows_of(t)
                    pe.wait_ge(s_sm, j + 1)
                    if j >= 1:
                        pe.wait_ge(s_oev, j)
                    o = bank(5)[0:r, 0:128]
                    last = mm(o, masked[0:r, j % 2, 0:r], vr[0:r, t, h, :], start=True, stop=(t == 0))
                    if t == LAST:
                        pe.wait_ge(s_state, 16)
                        last = mm(o, qhT[:, h, t * P:t * P + r], state_in[:, h, :], start=False, stop=True)
                    elif t > 0:
                        pe.wait_ge(s_U, (t - 1) * 4 + h + 1)
                        last = mm(o, qhT[:, h, t * P:t * P + r], U[:, t % 2, h, :], start=False, stop=True)
                    last.then_inc(s_ro, 1)

            for ev in events:
                if ev[0] == "proj":
                    proj(ev[1])
                elif ev[0] == "turn":
                    turn(*ev[1:])
                elif ev[0] == "adasum":
                    i = ev[1]
                    pe.wait_ge(s_acc, i + 1)
                    if i >= 2:
                        pe.wait_ge(s_rowo, i - 1)
                    mm(bank(5 + i % 2)[0:1, :], ones_col, ada_acc[:, i % 2], start=True, stop=True).then_inc(s_rsum, 1)
                elif ev[0] == "ret":
                    ret(ev[1])
            for n in (25, 26):
                pe.wait_ge(s_tre, n + 1)
            pe.wait_ge(s_freeA, 39)

            def cache_turn(n):
                pair, q = n // 4, n % 4
                pe.wait_ge(s_kc[0], 32 * (pair + 1))
                if n:
                    pe.wait_ge(s_kte, n)
                for j in range(4):
                    last = nc.tensor.transpose(bank(7)[:, j * P:(j + 1) * P],
                                               kc[:, 4 * q + j].rearrange("p h d -> p (h d)"), ident)
                last.then_inc(s_kt, 1)

            def qk(u):
                pair, a_, i, tl, first, _ = units[u]
                if u >= 3:
                    pe.wait_ge(s_sig, 2 * (u - 2))
                z = bank(u % 3)
                w = width(u)
                if i < LAST:
                    mm(z[:, 0:w], sqT[64 * a_:64 * a_ + 64, pair, i * P:(i + 1) * P],
                       skT[64 * a_:64 * a_ + 64, pair, tl[0] * P:tl[0] * P + w], start=True, stop=not first)
                    if first:
                        last = mm(z[:, w - P:w], half_ident, half_neg, start=False, stop=True)
                else:
                    for hh in range(2):
                        q = sqT[64 * hh:64 * hh + 64, pair, SEQ:SEQ + DEC]
                        zz = z[64 * hh:64 * hh + 64]
                        if first:
                            pe.wait_ge(s_kte, 4 * pair + 4)
                            mm(zz[:, 0:w - DEC], q, kTs[64 * hh:64 * hh + 64, tl[0] * P:PAST], start=True, stop=True)
                            mm(zz[:, w - DEC:w], q, skT[64 * hh:64 * hh + 64, pair, SEQ:SEQ + DEC],
                               start=False, stop=False, skip_group_check=True)
                        else:
                            mm(zz[:, 0:w], q, kTs[64 * hh:64 * hh + 64, tl[0] * P:tl[0] * P + w],
                               start=True, stop=True)
                    if first:
                        mm(z[:, w - DEC:w], half_ident, half_negs, start=False, stop=True, skip_group_check=True)
                pe_last[0].then_inc(s_qk, 1)

            def wturn(u):
                _, _, i, tl, _, _ = units[u]
                pe.wait_ge(s_wm, u + 1)
                if u >= 2:
                    pe.wait_ge(s_wte, u - 1)
                for j, t in enumerate(tl):
                    r = 64 if (i == LAST and t == 16) else P
                    last = nc.tensor.transpose(bank(3 + u % 2)[0:r, j * P:(j + 1) * P],
                                               wgt[:, u % 3, j * P:j * P + r], ident)
                last.then_inc(s_wt, 1)

            def pv(u):
                pair, a_, i, tl, first, lastu = units[u]
                o = outs_before[u]
                pe.wait_ge(s_wte, u + 1)
                if first and o >= 2:
                    pe.wait_ge(s_ov, ov_after[o - 2])
                ob = bank(5 + o % 2)
                for j, t in enumerate(tl):
                    st, sp_ = (first and j == 0), (lastu and j == len(tl) - 1)
                    if i < LAST:
                        last = mm(ob[:, 0:64], wT[:, u % 3, j, :], sv[:, t, (2 * pair + a_) * 64:(2 * pair + a_) * 64 + 64],
                                  start=st, stop=sp_)
                    elif t == 16:
                        last = mm(ob[:, 0:128], wT[0:64, u % 3, j, :], sv[0:64, LAST, pair * P:(pair + 1) * P],
                                  start=st, stop=sp_)
                    else:
                        if first and j == 0:
                            pe.wait_ge(s_kc[1], 32 * (pair + 1))
                        last = mm(ob[:, 0:128], wT[:, u % 3, j, :], vc[:, t].rearrange("p h d -> p (h d)"),
                                  start=st, stop=sp_)
                last.then_inc(s_pv, 1)

            for u in range(NU + 4):
                if u < NU:
                    lu = u % per_pair
                    if lu in (4, 8, 12, 16):
                        cache_turn(4 * (u // per_pair) + lu // 4 - 1)
                    qk(u)
                if 2 <= u < NU + 2:
                    wturn(u - 2)
                if u >= 4:
                    pv(u - 4)

            n = 0
            pe.wait_ge(s_wte, NU)
            pe.wait_ge(s_kte, 16)
            for half in range(2):
                for b, (t0, t1_) in enumerate(((0, 4), (4, 8), (8, 9))):
                    for k in range(4 * half, 4 * half + 4):
                        if half:
                            pe.wait_ge(s_sbn, t1_)
                        if n >= 4:
                            pe.wait_ge(s_meA if n - 4 < 12 else s_meD, (n - 4) % 12 + 1)
                        for t in range(t0, t1_):
                            r = rows_of(t)
                            c0 = (t - t0) * P
                            last = nc.tensor.transpose(bank(n % 4)[:, c0:c0 + r], mixed[0:r, t, k * P:(k + 1) * P],
                                                       ident[0:r, 0:r])
                        last.then_inc(s_mt, 1)
                        n += 1
            pe.wait_ge(s_ov, N_OUT + PAIRS)
            pe.wait_ge(s_meA, 12)
            pe.wait_ge(s_meD, 12)
            pe.wait_ge(s_wout, 16)

            def h2_turned(t):
                r = rows_of(t)
                pe.wait_ge(s_h2, t + 1)
                if t:
                    pe.wait_ge(s_hte, t)
                for k in range(KC):
                    last = nc.tensor.transpose(psum[2][:, k // 4, (k % 4) * P:(k % 4) * P + r],
                                               h2[0:r, t % 2, k * P:(k + 1) * P], ident[0:r, 0:r])
                last.then_inc(s_ht, 1)

            def logits(t):
                r = rows_of(t)
                pe.wait_ge(s_hte, t + 1)
                if t == 0:
                    pe.wait_ge(s_router, 64)
                for k in range(KC):
                    last = mm(bank(6)[0:r, t * 20:t * 20 + 20], h2T[:, k, 0:r], router_w[:, k, :],
                              start=(k == 0), stop=(k == KC - 1))
                last.then_inc(s_lg, 1)

            for t in range(TILES):
                r = rows_of(t)
                if t >= 2:
                    pe.wait_ge(s_ope, t - 1)
                for hh in range(2):
                    for k in range(KC):
                        last = mm(psum[t % 2][0:r, hh, :], mixT[:, k, t * P:t * P + r],
                                  wout[:, k, hh * 512:(hh + 1) * 512], start=(k == 0), stop=(k == KC - 1))
                    if hh == 1:
                        last.then_inc(s_op, 1)
                    elif t >= 3:
                        logits(t - 3)
                if t >= 2:
                    h2_turned(t - 2)
            logits(LAST - 2)
            for t in (LAST - 1, LAST):
                h2_turned(t)
                logits(t)
            pe.wait_ge(s_asg, 1)
            pe.wait_ge(s_ope, TILES)
            mm(bank(0)[:, 0:144], half_tri, Ab, start=True, stop=True)
            mm(bank(1)[:, 0:144], half_ones, Ab, start=True, stop=True).then_inc(s_rank, 1)

            for n in range(18):
                if n % 9 == 0:
                    pe.wait_ge(s_oh, n // 9 + 1)
                r = rows_of(n % 9)
                last = mm(bank(2)[:, 0:MAX_BLOCKS], place_oh[0:r, n, :], block_tok[0:r, n, :], start=(n == 0), stop=(n == 17))
            last.then_inc(s_ids, 1)

            def block_turn(b):
                pe.wait_ge(s_hg, 16 * (b + 1))
                for k in range(KC):
                    last = nc.tensor.transpose(psum[1][:, k // 4, (k % 4) * P:(k % 4 + 1) * P],
                                               hg[:, k * P:(k + 1) * P], ident)
                last.then_inc(s_htr, 1)

            pe.wait_ge(s_route, 1)
            block_turn(0)
            with pe.Fori(0, EXPERTS // 2) as ee:
                for k in range(2):
                    first = pe.value_load(table[0:1, bass.ds(2 * ee + k, 1)], min_val=0, max_val=MAX_BLOCKS - 1)
                    end = pe.value_load(table[0:1, bass.ds(2 * ee + k + 1, 1)], min_val=1, max_val=MAX_BLOCKS - 1)
                    for i in range(3):
                        pe.wait_ge(s_e[k][i], 16 * ee + 16)
                    pe.sem_inc(s_go, 1)
                    with pe.Fori(first, end) as b:
                        pe.wait_ge(s_hT, b + 1)
                        for f in range(FC):
                            pe.wait_ge(s_aT, 4 * b + f + 1)
                            for w in range(2):
                                for c in range(KC):
                                    last = mm(bank(f % 2)[:, w * P:(w + 1) * P], ew[k][w][:, c, f * P:(f + 1) * P],
                                              hTb[:, c, :], start=(c == 0), stop=(c == KC - 1))
                            last.then_inc(s_gu, 1)
                        pe.wait_ge(s_hg, 16 * b + 32)
                        for c in range(KC):
                            last = nc.tensor.transpose(psum[1][:, c // 4, (c % 4) * P:(c % 4 + 1) * P],
                                                       hg[:, c * P:(c + 1) * P], ident)
                        last.then_inc(s_htr, 1)
                        pe.wait_ge(s_ye, b + 1)
                        for f in range(FC):
                            pe.wait_ge(s_aT, 4 * b + f + 3)
                            for hh in range(2):
                                last = mm(psum[2][:, hh, :], aT[:, f, :], ew[k][2][:, f, hh * 512:(hh + 1) * 512],
                                          start=(f == 0), stop=(f == FC - 1))
                        last.then_inc(s_yp, 1)
                    nc.tensor.transpose(bank(7)[0:64, 0:64], ident[0:64, 0:64], ident[0:64, 0:64]).then_inc(s_edone, 1)

        @block.scalar
        def _(act):
            A = nc.scalar.activation
            act.wait_ge(s_colv, 1)
            A(csig, colv[:, 0:16], ACT.Sigmoid).then_inc(s_csig, 1)
            for j in range(4):
                act.wait_ge(s_adap, j + 1)
                A(ada_rows[0:2, j * 512:(j + 1) * 512], bank(6 + j % 2)[0:2, :], ACT.Copy).then_inc(s_adae, 1)
            act.wait_ge(s_mod, 1)
            n = 0
            for b, wd in enumerate((512, 512, DEC)):
                s = int(b == 2)
                for k in range(KC):
                    if n % 2 == 0:
                        act.wait_ge(s_lt, n + 1)
                        A(hT[:, k, b * 512:b * 512 + wd], bank(n % 4)[:, 0:wd], ACT.Identity,
                          bias=modv[:, s, k:k + 1], scale=modv[:, s, 8 + k:9 + k]).then_inc(s_leA, 1)
                    n += 1

            def turned(n, g, t):
                r = rows_of(t)
                dst = (qhT, khT, None, None, None, skT)[g]
                act.wait_ge(s_tr, n + 1)
                b = bank(3 if n % 2 == 0 else 7)
                A(dst[:, :, t * P:t * P + r], b.rearrange("p (h c) -> p h c", h=4)[:, :, 0:r], ACT.Copy).then_inc(s_tre, 1)

            for ev in events:
                if ev[0] == "proj":
                    k = ev[1]
                    g, t, ch = steps[k]
                    if g in (2, 3, 5, 6):
                        act.wait_ge(s_proj, k + 1)
                    r = rows_of(t)
                    b = bank(k % 3)
                    if g == 2:
                        A(vr[0:r, t].rearrange("p h d -> p (h d)"), b[0:r], ACT.Copy).then_inc(s_freeA, 1)
                    elif g == 3:
                        cw = 512 if ch < 2 else DEC
                        if (t, ch) == (0, 0):
                            act.wait_ge(s_rowo, 16)
                            for m in s_modw:
                                act.wait_ge(m, 128)
                        A(sqT[:, t, ch * 512:ch * 512 + cw], b[:, 0:cw], ACT.Copy).then_inc(s_freeA, 1)
                    elif g == 4:
                        act.wait_ge(s_proj, k + 1)
                        if t == 0:
                            act.wait_ge(s_so, 32)
                        if t >= 2:
                            act.wait_ge(s_gm, t - 1)
                        A(gate_sig[0:r, t % 2], b[0:r], ACT.Sigmoid).then_inc(s_gs, 1)
                    elif g == 5:
                        if t == 0:
                            act.wait_ge(s_mr, 9)
                        if t >= 2:
                            act.wait_ge(s_ko[t % 2], 16 * (t // 2))
                            act.wait_ge(s_tr, 18 + t - 1)
                        A(nat[t % 2][0:r].rearrange("p h d -> p (h d)"), b[0:r], ACT.Copy).then_inc(s_freeA, 1)
                    elif g == 6:
                        A(sv[0:r, t], b[0:r], ACT.Copy).then_inc(s_freeA, 1)
                elif ev[0] == "turn":
                    turned(*ev[1:])
                elif ev[0] == "adaout":
                    i = ev[1]
                    j, st = 4 + i // 2, i % 2
                    act.wait_ge(s_rowo, i + 1)
                    act.dma_start(mod_rows[j // 6, st:st + 1, (j % 6) * 512:(j % 6 + 1) * 512],
                                  row_out[0:1, i % 2]).then_inc(s_modw[i % 2], 16)
                elif ev[0] == "ret":
                    i = ev[1]
                    if i < 36:
                        t, h = ret_pos(i)
                        act.wait_ge(s_kv, i + 1)
                        if i >= 2:
                            act.wait_ge(s_U, i - 1)
                        if i == 0:
                            act.wait_ge(s_rope, 18)
                            act.wait_ge(s_tr, 18)
                        A(kvs[:, i % 2], bank(6)[:, 0:128], ACT.Copy, scale=gamma_chunk(t, h)).then_inc(s_kvs, 1)
                    if i >= 1:
                        j = i - 1
                        t, h = ret_pos(j)
                        r = rows_of(t)
                        act.wait_ge(s_ro, j + 1)
                        if j == 0:
                            act.wait_ge(s_rowo, 16)
                        A(mixed[0:r, t, h * P:(h + 1) * P], bank(5)[0:r, 0:128], ACT.Copy).then_inc(s_oev, 1)

            def squares(v):
                pair, a_, i, _, _, _ = units[v]
                o = outs_before[v]
                act.wait_ge(s_ov, ov_after[o])
                r = rows_of(i)
                for hh in ((a_,) if i < LAST else (0, 1)):
                    h = 2 * pair + hh
                    if s_sq_n[0]:
                        act.wait_ge(s_sq, s_sq_n[0])
                    s_sq_n[0] += 1
                    A(sq_junk[0:r], mixed[0:r, i, 512 + h * 64:512 + h * 64 + 64], ACT.Square,
                      accum_out=sb_sq[0:r, i, h:h + 1]).then_inc(s_sq, 1)

            s_sq_n = [0]
            for u in range(NU + 5):
                lu = u % per_pair
                if u < NU:
                    if lu in (4, 8, 12, 16):
                        n = 4 * (u // per_pair) + lu // 4 - 1
                        act.wait_ge(s_kt, n + 1)
                        A(kTs[:, (n % 4) * 512:(n % 4 + 1) * 512], bank(7), ACT.Copy).then_inc(s_kte, 1)
                    w = width(u)
                    act.wait_ge(s_qk, u + 1)
                    if u >= 3:
                        act.wait_ge(s_scan, u - 2)
                    A(om[:, u % 3, 0:w], bank(u % 3)[:, 0:w], ACT.Sigmoid, scale=-CHUNK_SCALE).then_inc(s_sig, 1)
                    if u >= 3:
                        act.wait_ge(s_wm, u - 2)
                    A(be[:, u % 3, 0:w], bank(u % 3)[:, 0:w], ACT.Sigmoid, scale=CHUNK_SCALE).then_inc(s_sig, 1)
                if 2 <= u < NU + 2:
                    weights_turned(act, u - 2)
                if u >= 5 and units[u - 5][5]:
                    squares(u - 5)

            n = 0
            for b, wd in enumerate((512, 512, DEC)):
                for k in range(4):
                    act.wait_ge(s_mt, n + 1)
                    A(mixT[:, k, b * 512:b * 512 + wd], bank(n % 4)[:, 0:wd], ACT.Copy,
                      scale=colv[:, 64 + k:65 + k]).then_inc(s_meA, 1)
                    n += 1
            for t in range(TILES + 2):
                v = t - 2
                if v >= 0:
                    r = rows_of(v)
                    act.wait_ge(s_ht, v + 1)
                    if v:
                        act.wait_ge(s_lg, v)
                    A(h2T[:, :, 0:r], psum[2].rearrange("p a (c q) -> p (a c) q", q=P)[:, :, 0:r], ACT.Copy).then_inc(s_hte, 1)
                if t < TILES:
                    r = rows_of(t)
                    act.wait_ge(s_nm1, t + 1)
                    A(t1[0:r, t % 2], t1[0:r, t % 2], ACT.Identity, bias=ln_nmr[0:r, t:t + 1],
                      scale=ln_rstd[0:r, t:t + 1]).then_inc(s_xh, 1)
                v = t - 1
                if 0 <= v < TILES:
                    r = rows_of(v)
                    act.wait_ge(s_nm2, v + 1)
                    if v >= 2:
                        act.wait_ge(s_h2o[v % 2], 16 * (v // 2))
                        act.wait_ge(s_ht, v - 1)
                    A(h2[0:r, v % 2], x1[0:r, v % 2], ACT.Identity, bias=ln_nmr[0:r, 9 + v:10 + v],
                      scale=ln_rstd[0:r, 9 + v:10 + v]).then_inc(s_h2a, 1)
            act.wait_ge(s_rt1, 1)
            A(gsub, gsub, ACT.Exp).then_inc(s_rt2, 1)
            act.wait_ge(s_rt1, 2)
            A(dd, dd, ACT.Exp).then_inc(s_rt2, 1)

            act.wait_ge(s_route, 1)
            act.wait_ge(s_h2o[0], 80)
            act.wait_ge(s_h2o[1], 64)
            act.wait_ge(s_htr, 1)
            A(hTb.rearrange("p (a c) q -> p a (c q)", a=2), psum[1][:], ACT.Copy).then_inc(s_hT, 1)
            act.sem_inc(s_ye, 1)
            act.sem_inc(s_ys, 16)
            with act.Fori(0, EXPERTS // 2) as ee:
                for k in range(2):
                    first = act.value_load(table[0:1, bass.ds(2 * ee + k, 1)], min_val=0, max_val=MAX_BLOCKS - 1)
                    end = act.value_load(table[0:1, bass.ds(2 * ee + k + 1, 1)], min_val=1, max_val=MAX_BLOCKS - 1)
                    with act.Fori(first, end) as b:
                        for f in range(FC):
                            act.wait_ge(s_gu, 4 * b + f + 1)
                            act.wait_ge(s_g1, 4 * b + f + 1)
                            A(sgb[:, f % 2], bank(f % 2)[:, 0:P], ACT.Sigmoid).then_inc(s_sg, 1)
                        act.wait_ge(s_htr, b + 2)
                        A(hTb.rearrange("p (a c) q -> p a (c q)", a=2), psum[1][:], ACT.Copy).then_inc(s_hT, 1)
                        act.wait_ge(s_yp, b + 1)
                        act.wait_ge(s_ys, 16 * b + 16)
                        A(yb.rearrange("p (a c) -> p a c", a=2), psum[2][:], ACT.Copy).then_inc(s_ye, 1)
                        act.wait_ge(s_ye, b + 2)
                        act.dma_start(y_dram[bass.ds(b * P, P), :], yb).then_inc(s_ys, 16)

            for t in range(TILES + 2):
                if t < TILES:
                    r = rows_of(t)
                    act.wait_ge(s_y0[t], 32)
                    A(ya[t][0:r], ya[t][0:r], ACT.Copy, scale=w0[0:r, t:t + 1]).then_inc(s_crs, 1)
                v = t - 2
                if v >= 0:
                    r = rows_of(v)
                    act.wait_ge(s_cnm, v + 1)
                    A(ya[v][0:r], ya[v][0:r], ACT.Identity, bias=ln_nmr[0:r, v:v + 1],
                      scale=ln_rstd[0:r, v:v + 1]).then_inc(s_cxh, 1)

        @block.vector
        def _(dve):
            V = nc.vector
            step = Steps(dve, s_dv)
            TT, TS, STT = V.tensor_tensor, V.tensor_scalar, V.scalar_tensor_tensor

            def done(ins, s, value):
                ins.then_inc(s, 1)
                dve.wait_ge(s, value)

            step(V.memset(mhalf, -0.5))
            step(V.memset(half_ones, 1.0))
            step(V.memset(ones_col, 1.0))
            step(V.memset(ret_stats, 0.0))
            dve.wait_ge(s_const, 16)
            step(V.tensor_copy(half_ident, ident))
            step(V.tensor_copy(half_neg, cst[:, C_NEG:C_NEG + 128]))
            step(V.tensor_copy(half_negs, cst[:, C_NEGS:C_NEGS + 64]))
            step(V.tensor_copy(half_tri, cst[:, C_TRI:C_TRI + 128]))
            dve.wait_ge(s_rowT, 1)
            done(V.tensor_copy(colv, bank(7)[:, 0:72]), s_colv, 1)

            def variance(src, r, dst):
                for hh in range(2):
                    step(V.bn_stats(stats[0:r, hh, :], src[:, hh * 512:(hh + 1) * 512]))
                step(V.bn_aggr(dst, stats[0:r].rearrange("p a b -> p (a b)")))

            def batch_ln(b, t0, t1_):
                dve.wait_ge(s_xb[b], 16)
                for t in range(t0, t1_):
                    variance(xt[0:rows_of(t), t, :], rows_of(t), mv[0:rows_of(t), t, :])
                r = rows_of(t0)
                done(TS(ve[0:r, t0:t1_], mv[0:r, t0:t1_, 1], EPS, None, ALU.add), s_ve, b + 1)
                dve.wait_ge(s_rstd, b + 1)
                step(STT(nmr[0:r, t0:t1_], mv[0:r, t0:t1_, 0], -1.0, rstd[0:r, t0:t1_], ALU.mult, ALU.mult))
                for t in range(t0, t1_):
                    x = xt[0:r, t, :]
                    done(TS(x, x, rstd[0:r, t:t + 1], nmr[0:r, t:t + 1], ALU.mult, ALU.add), s_xn, t + 1)

            dve.wait_ge(s_csig, 1)
            TT(silu_c.rearrange("p k s -> p s k"), colv[:, 0:16].rearrange("p (s k) -> p s k", s=2),
               csig.rearrange("p (s k) -> p s k", s=2), ALU.mult).then_inc(s_silu, 1)
            batch_ln(0, 0, 4)
            batch_ln(1, 4, 8)
            batch_ln(2, 8, 9)

            dve.wait_ge(s_adat, 4)
            step(TT(modv, bank(5)[:, 0:32].rearrange("p (e s) -> p s e", s=2),
                    colv[:, 16:32].unsqueeze(1).to_broadcast([P, 2, 16]), ALU.add))
            done(TS(modv[:, :, 8:16], modv[:, :, 8:16], 1.0, None, ALU.add), s_mod, 1)
            n = 0
            for b, wd in enumerate((512, 512, DEC)):
                s = int(b == 2)
                for k in range(KC):
                    if n % 2 == 1:
                        dve.wait_ge(s_lt, n + 1)
                        TS(hT[:, k, b * 512:b * 512 + wd], bank(n % 4)[:, 0:wd], modv[:, s, 8 + k:9 + k],
                           modv[:, s, k:k + 1], ALU.mult, ALU.add).then_inc(s_leD, 1)
                    n += 1

            def ret(i):
                if i >= 36:
                    return
                t, h = ret_pos(i)
                r = rows_of(t)
                dve.wait_ge(s_sc, i + 1)
                if i == 0:
                    dve.wait_ge(s_rope, 18)
                    dve.wait_ge(s_tr, 18)
                if i >= 2:
                    dve.wait_ge(s_ro, i - 1)
                TT(masked[0:r, i % 2, 0:r], bank(4)[0:r, 0:r], cst[0:r, C_CAUSAL:C_CAUSAL + r], ALU.mult).then_inc(s_sm, 1)
                dve.wait_ge(s_kvs, i + 1)
                if t == 0:
                    done(V.tensor_copy(U[:, 1, h, :], kvs[:, i % 2]), s_U, i + 1)
                elif t == LAST:
                    dve.wait_ge(s_state, 16)
                    done(STT(state_out[:, h, :], state_in[:, h, :], gamma_chunk(t, h), kvs[:, i % 2], ALU.mult, ALU.add),
                         s_U, i + 1)
                else:
                    dve.wait_ge(s_ro, (t - 1) * 4 + h + 1)
                    done(STT(U[:, (t + 1) % 2, h, :], U[:, t % 2, h, :], gamma_chunk(t, h), kvs[:, i % 2],
                             ALU.mult, ALU.add), s_U, i + 1)

            for ev in events:
                if ev[0] == "proj":
                    k = ev[1]
                    g, t, ch = steps[k]
                    r = rows_of(t)
                    b = bank(k % 3)[0:r].rearrange("p (h d) -> p h d", h=4)
                    if g < 2:
                        n = free_count[k][1]
                        dve.wait_ge(s_rot, 16)
                        dve.wait_ge(s_proj, k + 1)
                        if n > 1:
                            dve.wait_ge(s_rc, n - 1)
                        b4 = b.rearrange("p h (a d) -> p h a d", a=2)
                        cos = rot[0:r, 64 * t:64 * t + 64].unsqueeze(1).unsqueeze(1).to_broadcast([r, 4, 2, 64])
                        sin = rot[0:r, 64 * TILES + 128 * t:64 * TILES + 128 * t + 128].rearrange("p (a d) -> p a d", a=2)\
                            .unsqueeze(1).to_broadcast([r, 4, 2, 64])
                        TT(rope_a[0:r].rearrange("p h (a d) -> p h a d", a=2), b4, cos, ALU.mult).then_inc(s_ra, 1)
                        done(TT(rope_b[0:r].rearrange("p h (a d) -> p h a d", a=2), b4[:, :, ::-1, :], sin, ALU.mult),
                             s_freeD, n)
                        dve.wait_ge(s_ra, n)
                    elif g == 4:
                        n = free_count[k][1]
                        dve.wait_ge(s_gs, t + 1)
                        if t >= 2:
                            dve.wait_ge(s_mr, t - 1)
                        done(TT(gate_lin[0:r, t % 2], gate_sig[0:r, t % 2], bank(k % 3)[0:r], ALU.mult), s_freeD, n)
                        m4 = mixed[0:r, t, 0:512].rearrange("p (h d) -> p h d", h=4)
                        step(TT(m4, m4, rstd_b[0:r, 4 * t:4 * t + 4].unsqueeze(2).to_broadcast([r, 4, 128]), ALU.mult))
                        done(TT(m4, m4, ret_m[0:r, 4 * t:4 * t + 4].unsqueeze(2).to_broadcast([r, 4, 128]), ALU.add),
                             s_gm, t + 1)
                elif ev[0] == "adaout":
                    i = ev[1]
                    j = 4 + i // 2
                    dve.wait_ge(s_rsum, i + 1)
                    dve.wait_ge(s_bias[j % 2], 16 * ((j - 4) // 2 + 1))
                    if i >= 2:
                        dve.wait_ge(s_modw[i % 2], 16 * (i // 2))
                    done(STT(row_out[0:1, i % 2], bank(5 + i % 2)[0:1, :], 1.0 if j in (8, 9) else 0.0,
                             bias_row[0:1, j % 2], ALU.add, ALU.add), s_rowo, i + 1)
                elif ev[0] == "ada":
                    i = ev[1]
                    j, st = 4 + i // 2, i % 2
                    dve.wait_ge(s_adaM[j % 2], 16 * ((j - 4) // 2 + 1))
                    if i >= 2:
                        dve.wait_ge(s_rsum, i - 1)
                    w, o = ada_m[j % 2], ada_acc[:, i % 2]
                    step(TS(o, w[:, 0], silu_c[:, 0, st:st + 1], None, ALU.mult))
                    for k in range(1, KC - 1):
                        step(STT(o, w[:, k], silu_c[:, k, st:st + 1], o, ALU.mult, ALU.add))
                    done(STT(o, w[:, KC - 1], silu_c[:, KC - 1, st:st + 1], o, ALU.mult, ALU.add), s_acc, i + 1)
                elif ev[0] == "ret":
                    ret(ev[1])
                elif ev[0] == "retfin":
                    for i in range(36):
                        t, h = ret_pos(i)
                        dve.wait_ge(s_oev, i + 1)
                        r = rows_of(t)
                        last = V.bn_stats(ret_stats[0:r, i, :], mixed[0:r, t, h * P:(h + 1) * P])
                        if i < 35:
                            last.then_inc(s_dv, 1)
                            step.n += 1
                    step(last)
                    step(TT(ret_m, ret_stats[:, :, 1], ret_stats[:, :, 4], ALU.add))
                    step(TT(ret_d, ret_stats[:, :, 1], ret_stats[:, :, 4], ALU.subtract))
                    step(TT(ve, ret_stats[:, :, 2], ret_stats[:, :, 5], ALU.add))
                    step(TS(ve, ve, 1.0 / 128, EPS, ALU.mult, ALU.add))
                    step(STT(ret_d, ret_d, 0.25, ret_d, ALU.mult, ALU.mult))
                    done(TT(ve, ve, ret_d, ALU.add), s_rve, 1)
                    dve.wait_ge(s_rrs, 1)
                    step(STT(ret_m, ret_m, -0.5, rstd_b, ALU.mult, ALU.mult))

            dve.wait_ge(s_mr, 9)
            dve.wait_ge(s_ro, 36)
            step(V.memset(sb_sq, 1.0))
            done(V.memset(pf[:, :, 512:513], 1.0), s_ones, 1)
            for u in range(NU + 4):
                if u < NU:
                    w = width(u)
                    pb = scan_buf(u)
                    o = om[:, u % 3, 0:w]
                    dve.wait_ge(s_sig, 2 * u + 1)
                    if not units[u][4]:
                        prev = scan_buf(u - 1)
                        pw = 512 - width(u - 1)
                        step(V.tensor_copy(pb[:, 512:513], prev[:, pw:pw + 1]))
                        init = pb[:, 512:513]
                    else:
                        init = 1.0
                    lo = 512 - w
                    pbr = pb[:, 511:lo - 1:-1] if lo > 0 else pb[:, 511::-1]
                    done(V.tensor_tensor_scan(pbr, om[:, u % 3, w - 1::-1], om[:, u % 3, w - 1::-1], init,
                                              ALU.mult, ALU.min), s_scan, u + 1)
                    dve.wait_ge(s_sig, 2 * u + 2)
                    if u >= 3:
                        dve.wait_ge(s_wt, u - 2)
                    done(TT(wgt[:, u % 3, 0:w], be[:, u % 3, 0:w], pb[:, lo + 1:513], ALU.mult), s_wm, u + 1)
                if u >= 4 and units[u - 4][5]:
                    v = u - 4
                    pair, a_, i, _, _, _ = units[v]
                    ob = bank(5 + outs_before[v] % 2)
                    dve.wait_ge(s_pv, v + 1)
                    if i < LAST:
                        V.tensor_copy(mixed[:, i, 512 + (2 * pair + a_) * 64:512 + (2 * pair + a_) * 64 + 64],
                                      ob[:, 0:64]).then_inc(s_ov, 1)
                    else:
                        for hh in range(2):
                            V.tensor_copy(mixed[0:64, LAST, 512 + (2 * pair + hh) * 64:512 + (2 * pair + hh) * 64 + 64],
                                          ob[64 * hh:64 * hh + 64, 64 * hh:64 * hh + 64]).then_inc(s_ov, 1)
            dve.wait_ge(s_ov, N_OUT + PAIRS)
            dve.wait_ge(s_sq, N_OUT + PAIRS)
            done(TS(sb_sq, sb_sq, 1.0 / 64, EPS, ALU.mult, ALU.add), s_sbv, 1)
            dve.wait_ge(s_sbr, 1)
            for t in range(TILES):
                r = rows_of(t)
                m83 = mixed[0:r, t, 512:1024].rearrange("p (h d) -> p h d", h=8)
                TT(m83, m83, sb_rstd[0:r, t].unsqueeze(2).to_broadcast([r, 8, 64]), ALU.mult).then_inc(s_sbn, 1)
            n = 12
            for b, wd in enumerate((512, 512, DEC)):
                for k in range(4, KC):
                    dve.wait_ge(s_mt, n + 1)
                    TS(mixT[:, k, b * 512:b * 512 + wd], bank(n % 4)[:, 0:wd], colv[:, 64 + k:65 + k], None,
                       ALU.mult).then_inc(s_meD, 1)
                    n += 1

            def variance_out(x, r, col, s, value):
                variance(x, r, ln_mv[0:r, col, :])
                done(TS(ln_ve[0:r, col:col + 1], ln_mv[0:r, col, 1:2], EPS, None, ALU.add), s, value)

            dve.wait_ge(s_brow, 128)
            for t in range(TILES + 1):
                if t < TILES:
                    r = rows_of(t)
                    s = int(t == LAST)
                    x = t1[0:r, t % 2]
                    dve.wait_ge(s_op, t + 1)
                    done(TT(x, psum[t % 2][0:r].rearrange("p a b -> p (a b)"), rows5[0:r, s], ALU.mult), s_ope, t + 1)
                    dve.wait_ge(s_x5[t % 2], 16 * (t // 2 + 1))
                    step(STT(x, xin[0:r, t % 2], ALPHA, x, ALU.mult, ALU.add))
                    variance_out(x, r, t, s_ve1, t + 1)
                v = t - 1
                if v >= 0:
                    r = rows_of(v)
                    x = t1[0:r, v % 2]
                    dve.wait_ge(s_xh, v + 1)
                    step(TT(x, x, rows5[0:r, 6], ALU.mult))
                    if v >= 2:
                        dve.wait_ge(s_x1o[v % 2], 16 * (v // 2))
                        dve.wait_ge(s_h2a, v - 1)
                    done(TT(x1[0:r, v % 2], x, rows5[0:r, 7], ALU.add), s_x1, v + 1)
                    variance_out(x1[0:r, v % 2], r, 9 + v, s_ve2, v + 1)

            dve.wait_ge(s_lg, 9)
            step(V.memset(lg, 0.0))
            step(TT(lg[:, 0:8], bank(6)[:, 0:160].rearrange("p (t n) -> p t n", t=8),
                    router_b.unsqueeze(1).to_broadcast([P, 8, 20]), ALU.add))
            step(TT(lg[0:DEC, 8], bank(6)[0:DEC, 160:180], router_b[0:DEC], ALU.add))
            firsts = cst[:, C_FIRST:C_FIRST + 4].unsqueeze(1).to_broadcast([P, 9, 4])

            def wide(v, n_=4):
                return v.unsqueeze(2).to_broadcast([P, 9, n_])

            def first_max(src, mx, dst):
                step(V.tensor_reduce(mx, src, AX.X, ALU.max))
                step(TT(eq, src, wide(mx), ALU.is_equal))
                step(TT(eq, eq, firsts, ALU.mult))
                step(V.tensor_reduce(eqm, eq, AX.X, ALU.max))
                step(TT(dst, eq, wide(eqm), ALU.is_equal))

            g4 = lg[:, :, 0:4]
            first_max(g4, gmax, oh)
            done(TT(gsub, g4, wide(gmax), ALU.subtract), s_rt1, 1)
            step(TT(oh, oh, wide(cst[:, C_VALID:C_VALID + 9]), ALU.mult))
            p4 = prod.rearrange("p t (g j) -> p t g j", g=4)
            for g in range(4):
                step(TT(p4[:, :, g, :], lg[:, :, 4 + 4 * g:8 + 4 * g], oh[:, :, g:g + 1].to_broadcast([P, 9, 4]), ALU.mult))
            step(V.tensor_reduce(ein, p4.rearrange("p t g j -> p t j g"), AX.X, ALU.add))
            first_max(ein, v0, a0)
            step(STT(ein, a0, NEG, ein, ALU.mult, ALU.add))
            first_max(ein, v1, a1)
            dve.wait_ge(s_rt2, 1)
            done(TT(dd, v1, v0, ALU.subtract), s_rt1, 2)
            step(V.tensor_reduce(gsum, gsub, AX.X, ALU.add))
            dve.wait_ge(s_rt2, 2)
            step(TS(w1, dd, 1.0, None, ALU.add))
            step(TT(gsum, gsum, w1, ALU.mult))
            step(V.reciprocal(w0, gsum))
            step(TT(w1, w0, dd, ALU.mult))
            for A_, a_ in ((A0, a0), (A1, a1)):
                for g in range(4):
                    step(TT(A_.rearrange("p t (g j) -> p t g j", g=4)[:, :, g, :], a_,
                            oh[:, :, g:g + 1].to_broadcast([P, 9, 4]), ALU.mult))
            done(TT(Ab.rearrange("p (t e) -> p t e", t=9), A0, A1, ALU.add), s_asg, 1)
            dve.wait_ge(s_rank, 1)
            step(V.tensor_copy(tot, bank(1)[:, 0:144].rearrange("p (t e) -> p t e", t=9)))
            step(V.memset(prior[:, 0], 0.0))
            for t in range(1, 9):
                step(TT(prior[:, t], prior[:, t - 1], tot[:, t - 1], ALU.add))
            step(TT(cnt16, prior[:, 8], tot[:, 8], ALU.add))
            step(TT(cmp8, cnt16.unsqueeze(2).to_broadcast([P, 16, 8]),
                    cst[:, C_LIMIT:C_LIMIT + 8].unsqueeze(1).to_broadcast([P, 16, 8]), ALU.is_gt))
            step(V.tensor_reduce(nb, cmp8, AX.X, ALU.add))
            step(TS(nb, nb, 1.0, None, ALU.add))
            step(V.tensor_tensor_scan(incl, nb, nb, 0.0, ALU.add, ALU.max))
            step(V.memset(table_f, 0.0))
            step(V.tensor_copy(table_f[:, 1:17], incl))
            step(V.tensor_copy(table, table_f))
            step(TS(cnt16, table_f[:, 0:16], 128.0, None, ALU.mult))
            step(TT(slots, bank(0)[:, 0:144].rearrange("p (t e) -> p t e", t=9), prior, ALU.add))
            step(TT(slots, slots, cnt16.unsqueeze(1).to_broadcast([P, 9, 16]), ALU.add))
            for kk, A_ in enumerate((A0, A1)):
                step(TT(A_, A_, slots, ALU.mult))
                step(V.tensor_reduce(sk_f[:, kk], A_, AX.X, ALU.add))
            slot = sk_f.rearrange("p a t -> p (a t)")
            dve.wait_ge(s_iota, 3)
            step(TT(past, slot.unsqueeze(2).to_broadcast([P, 18, MAX_BLOCKS + 1]),
                    starts.unsqueeze(1).to_broadcast([P, 18, MAX_BLOCKS + 1]), ALU.is_ge))
            step(TT(block_oh, past[:, :, 0:MAX_BLOCKS], past[:, :, 1:MAX_BLOCKS + 1], ALU.subtract))
            step(V.tensor_reduce(slot_block, past[:, :, 1:MAX_BLOCKS + 1], AX.X, ALU.add))
            step(STT(slot_place, slot_block, -128.0, slot, ALU.mult, ALU.add))
            for kk in range(2):
                step(TT(block_tok[:, 9 * kk:9 * kk + 9], block_oh[:, 9 * kk:9 * kk + 9],
                        tok_f.unsqueeze(2).to_broadcast([P, 9, MAX_BLOCKS]), ALU.mult))
            for kk in range(2):
                done(TT(place_oh[:, 9 * kk:9 * kk + 9], slot_place[:, 9 * kk:9 * kk + 9].unsqueeze(2).to_broadcast([P, 9, P]),
                        places.unsqueeze(1).to_broadcast([P, 9, P]), ALU.is_equal), s_oh, kk + 1)
            step(V.memset(zero_rows, 0.0))
            done(V.tensor_copy(slot_i, sk_f), s_route, 1)
            dve.wait_ge(s_ids, 1)
            done(V.tensor_copy(gi, bank(2)[:, 0:MAX_BLOCKS]), s_gi, 1)
            dve.sem_inc(s_aT, 2)
            dve.sem_inc(s_g1, 2)
            with dve.Fori(0, EXPERTS // 2) as ee:
                for k in range(2):
                    first = dve.value_load(table[0:1, bass.ds(2 * ee + k, 1)], min_val=0, max_val=MAX_BLOCKS - 1)
                    end = dve.value_load(table[0:1, bass.ds(2 * ee + k + 1, 1)], min_val=1, max_val=MAX_BLOCKS - 1)
                    with dve.Fori(first, end) as b:
                        for f in range(FC):
                            dve.wait_ge(s_sg, 4 * b + f + 1)
                            TT(g1b[:, f % 2], sgb[:, f % 2], bank(f % 2)[:, 0:P], ALU.mult).then_inc(s_g1, 1)
                            dve.wait_ge(s_g1, 4 * b + f + 3)
                            TT(aT[:, f], g1b[:, f % 2], bank(f % 2)[:, P:2 * P], ALU.mult).then_inc(s_aT, 1)
                            dve.wait_ge(s_aT, 4 * b + f + 3)

            dve.wait_ge(s_frow, 64)
            dve.wait_ge(s_x1i, 16 * TILES)
            for t in range(TILES + 2):
                if t < TILES:
                    r = rows_of(t)
                    x = ya[t][0:r]
                    dve.wait_ge(s_crs, t + 1)
                    step(STT(x, yc[t][0:r], w1[0:r, t:t + 1], x, ALU.mult, ALU.add))
                    step(TT(x, x, rows8[0:r, int(t == LAST)], ALU.mult))
                    done(STT(x, x1c[t][0:r], ALPHA, x, ALU.mult, ALU.add), s_cacc, t + 1)
                    variance_out(x, r, t, s_cve, t + 1)
                v = t - 2
                if v >= 0:
                    r = rows_of(v)
                    dve.wait_ge(s_cxh, v + 1)
                    TT(ya[v][0:r], ya[v][0:r], rows8[0:r, 2], ALU.mult).then_inc(s_cg, 1)

        @block.gpsimd
        def _(pool):
            G = nc.gpsimd
            step = Steps(pool, s_po)
            step(G.iota(tok_i, [[P, 9]], base=0, channel_multiplier=1))
            for b, (t0, t1_) in enumerate(((0, 4), (4, 8), (8, 9))):
                r = rows_of(t0)
                pool.wait_ge(s_ve, b + 1)
                G.tensor_tensor(rstd[0:r, t0:t1_], ve[0:r, t0:t1_], mhalf[0:r, t0:t1_], ALU.pow).then_inc(s_rstd, 1)
            n = 0
            for ev in events:
                if ev[0] == "proj":
                    g, t, _ = steps[ev[1]]
                    r = rows_of(t)
                    if g < 2:
                        n += 1
                        pool.wait_ge(s_freeD, n)
                        pool.wait_ge(s_ra, n)
                        G.tensor_tensor(rope_c[0:r], rope_a[0:r], rope_b[0:r], ALU.add).then_inc(s_rc, 1)
                        pool.wait_ge(s_rc, n)
                        if g == 0 and t >= 2:
                            pool.wait_ge(s_tr, t - 1)
                        c = (C_GQ, C_GK)[g]
                        dst = nat[t % 2] if g == 0 else kh[:, t]
                        G.tensor_tensor(dst[0:r], rope_c[0:r], cst[0:r, c:c + 4].unsqueeze(2).to_broadcast([r, 4, 128]),
                                        ALU.mult).then_inc(s_rope, 1)
                        pool.wait_ge(s_rope, n)
                    elif g == 4:
                        pool.wait_ge(s_gm, t + 1)
                        m = mixed[0:r, t, 0:512]
                        G.tensor_tensor(m, m, gate_lin[0:r, t % 2], ALU.mult).then_inc(s_mr, 1)
                elif ev[0] == "retfin":
                    pool.wait_ge(s_rve, 1)
                    G.tensor_tensor(rstd_b, ve, mhalf, ALU.pow).then_inc(s_rrs, 1)
            pool.wait_ge(s_sbv, 1)
            G.tensor_tensor(sb_rstd, sb_sq, mhalf[:, 0:1].unsqueeze(2).to_broadcast([P, 9, 8]), ALU.pow).then_inc(s_sbr, 1)
            for t in range(TILES + 1):
                if t < TILES:
                    pool.wait_ge(s_ve1, t + 1)
                    norm_scalars(step, G, rows_of(t), t).then_inc(s_nm1, 1)
                v = t - 1
                if v >= 0:
                    r = rows_of(v)
                    s = int(v == LAST)
                    pool.wait_ge(s_ve2, v + 1)
                    norm_scalars(step, G, r, 9 + v).then_inc(s_nm2, 1)
                    pool.wait_ge(s_h2a, v + 1)
                    h = h2[0:r, v % 2]
                    step(G.tensor_tensor(h, h, rows5[0:r, 2 + s], ALU.mult))
                    G.tensor_tensor(h, h, rows5[0:r, 4 + s], ALU.add).then_inc(s_h2, 1)
            pool.wait_ge(s_h2, TILES)
            G.iota(starts_i, [[P, MAX_BLOCKS + 1]], base=0, channel_multiplier=0).then_inc(s_po, 1)
            G.iota(places_i, [[1, P]], base=0, channel_multiplier=0).then_inc(s_po, 1)
            step.n += 2
            pool.wait_ge(s_po, step.n)
            G.tensor_copy(starts, starts_i).then_inc(s_iota, 1)
            G.tensor_copy(places, places_i).then_inc(s_iota, 1)
            G.tensor_copy(tok_f, tok_i).then_inc(s_iota, 1)
            pool.wait_ge(s_route, 1)
            pool.wait_ge(s_gi, 1)
            pool.wait_ge(s_h2o[0], 80)
            pool.wait_ge(s_h2o[1], 64)
            total = pool.value_load(table[0:1, 16:17], min_val=1, max_val=MAX_BLOCKS - 1)
            G.tensor_copy(idc, gi[:, 0:1]).then_inc(s_idx, 1)
            pool.wait_ge(s_idx, 1)
            pool.indirect_dma_start(hg, None, h2_dram, bass.IndirectOffsetOnAxis(ap=idc[:, 0:1], axis=0)).then_inc(s_hg, 16)
            with pool.Fori(1, total + 1) as b:
                pool.wait_ge(s_htr, b)
                pool.wait_ge(s_hg, 16 * b)
                pool.sem_inc(s_fill, 16)
                G.tensor_copy(idc, gi[:, bass.ds(b, 1)]).then_inc(s_idx, 1)
                pool.wait_ge(s_idx, b + 1)
                pool.sem_inc(s_go, 1)
                pool.indirect_dma_start(hg, None, h2_dram, bass.IndirectOffsetOnAxis(ap=idc[:, 0:1], axis=0)).then_inc(s_hg, 16)
            pool.wait_ge(s_fill, 16 * MAX_BLOCKS)
            pool.wait_ge(s_ys, 16 * total + 16)
            pool.sem_inc(s_go, 1)
            pool.wait_ge(s_edone, EXPERTS)
            pool.sem_inc(s_go, 1)

            def gather(t):
                r = rows_of(t)
                for kk, dst in enumerate((ya[t], yc[t])):
                    pool.indirect_dma_start(dst[0:r], None, y_dram,
                                            bass.IndirectOffsetOnAxis(ap=slot_i[0:r, kk, t:t + 1], axis=0)).then_inc(s_y0[t], 16)

            for t in range(3):
                gather(t)
            pool.wait_ge(s_frow, 64)
            for t in range(TILES + 2):
                if t + 3 < TILES:
                    gather(t + 3)
                if t < TILES:
                    pool.wait_ge(s_cve, t + 1)
                    norm_scalars(step, G, rows_of(t), t).then_inc(s_cnm, 1)
                v = t - 2
                if v >= 0:
                    r = rows_of(v)
                    pool.wait_ge(s_cg, v + 1)
                    G.tensor_tensor(ya[v][0:r], ya[v][0:r], rows8[0:r, 3], ALU.add).then_inc(s_cy, 1)


def launch_shapes():
    return [("y_prompt", (1, SEQ, D)), ("y_sample", (1, DEC, D)), ("k_prompt", (1, 1, SB_HEADS, SEQ, HD)),
            ("v_prompt", (1, 1, SB_HEADS, SEQ, HD)), ("state_prompt", (1, 1, RET_HEADS, 128, 128)),
            ("k_sample", (1, 1, SB_HEADS, DEC, HD)), ("v_sample", (1, 1, SB_HEADS, DEC, HD)),
            ("state_sample", (1, 1, RET_HEADS, 128, 128))]


_INS = ['x_prompt', 'x_sample', 'cache_sb_k', 'cache_sb_v', 'state_ret', 'c_prompt', 'c_sample', 'w_in', 'w_out',
        'ret_norm_g', 'sb_norm_g', 'w_ada_mix', 'b_ada_mix', 'ln_mix_g', 'ln_mix_b', 'w_ada_ffn', 'b_ada_ffn',
        'ln_ffn_g', 'ln_ffn_b', 'w_group', 'b_group', 'w_router', 'b_router', 'w_e_gate', 'w_e_up', 'w_e_down']


def kernel(**inputs):
    import concourse.bacc as _bacc
    from concourse.bass_utils import run_bass_kernel_spmd as _run

    nc = _bacc.Bacc("TRN2", target_bir_lowering=False, num_devices=1)
    arrays, args = {}, []
    for name in _INS:
        arr = np.ascontiguousarray(inputs[name])
        arrays[f"in_{name}"] = arr
        args.append(nc.dram_tensor(f"in_{name}", arr.shape, mybir.dt.from_np(arr.dtype), kind="ExternalInput").ap())
    arrays["in_consts"] = shape_constants()
    args.append(nc.dram_tensor("in_consts", (P, C_END), F32, kind="ExternalInput").ap())
    for name, shape in launch_shapes():
        args.append(nc.dram_tensor(f"out_{name}", shape, F32, kind="ExternalOutput").ap())
    for name, shape, dt in (("mod_rows", (2, 2, 3 * D), F32), ("x1_rows", (TOK, D), F32), ("h2_rows", (TOK, D), F32),
                            ("expert_rows", (MAX_BLOCKS * P, D), F32)):
        args.append(nc.dram_tensor(name, shape, dt, kind="Internal").ap())
    stream_step(nc, args)
    r = _run(nc, [arrays], core_ids=[0])
    return tuple(r.results[0][f"out_{name}"] for name, _ in launch_shapes())
```

```python
from contextlib import ExitStack

import numpy as np

import concourse.bass as bass
from concourse import mybir

ALU = mybir.AluOpType
ACT = mybir.ActivationFunctionType
AX = mybir.AxisListType
F32 = mybir.dt.float32
F32R = mybir.dt.float32r
BF16 = mybir.dt.bfloat16
I32 = mybir.dt.int32

P = 128
D = 1024
KC = D // P
SEQ = 1024
DEC = 64
PAST = 2048
TILES = SEQ // P + 1
LAST = TILES - 1
TOK = SEQ + DEC
RET_HEADS = 4
SB_HEADS = 8
PAIRS = SB_HEADS // 2
HD = 64
EXPERTS = 16
F = 512
FC = F // P
ALPHA = 2.0 ** 0.25
EPS = 1e-5
NEG = -1.0e30
CHUNK_SCALE = HD ** -0.5
MAX_BLOCKS = 33
ARENA = 53104
SMALLS = 608 + 1552 + 2560
EXPERT_W = 2 * KC * F + FC * D
LOG_GAMMA = np.log1p(-np.exp2(-5.0 - np.arange(RET_HEADS)))
STEPS_BEFORE = [0, 9, 18, 27, 39, 48, 57, 66]

C_IDENT = 0
C_CAUSAL = 128
C_NEG = C_CAUSAL + 128
C_NEGS = C_NEG + 128
C_GQ = C_NEGS + 64
C_GK = C_GQ + 4
C_TRI = C_GK + 4
C_FIRST = C_TRI + 128
C_VALID = C_FIRST + 4
C_LIMIT = C_VALID + TILES
C_MAIN = C_LIMIT + 8
C_COS = C_MAIN
C_SIN = C_COS + TILES * 64
C_END = C_SIN + TILES * 128


def shape_constants():
    c = np.zeros((P, C_END), np.float32)
    i = np.arange(P)
    c[:, C_IDENT:C_IDENT + 128] = np.eye(P)
    inv = np.float32(10000.0) ** (-np.arange(64, dtype=np.float32) / np.float32(64))
    for t in range(TILES):
        pos = (i + t * P if t < LAST else PAST + i).astype(np.float32)
        ang = (pos[:, None] * inv[None, :]).astype(np.float64)
        c[:, C_COS + 64 * t:C_COS + 64 * t + 64] = np.cos(ang)
        c[:, C_SIN + 128 * t:C_SIN + 128 * t + 64] = -np.sin(ang)
        c[:, C_SIN + 128 * t + 64:C_SIN + 128 * t + 128] = np.sin(ang)
    c[:, C_CAUSAL:C_CAUSAL + 128] = i[:, None] <= i[None, :]
    c[:, C_NEG:C_NEG + 128] = np.where(i[None, :] >= i[:, None], NEG, 0.0)
    c[:, C_NEGS:C_NEGS + 64] = np.where(i[None, :64] >= (i % 64)[:, None], NEG, 0.0)
    for h in range(RET_HEADS):
        c[:, C_GQ + h] = np.exp(LOG_GAMMA[h] * (i + 1))
        c[:, C_GK + h] = np.exp(-LOG_GAMMA[h] * (i + 1)) * 128.0 ** -0.5
    c[:, C_TRI:C_TRI + 128] = i[:, None] < i[None, :]
    c[:, C_FIRST:C_FIRST + 4] = [4, 3, 2, 1]
    c[:, C_VALID:C_VALID + TILES] = 1.0
    c[64:, C_VALID + LAST] = 0.0
    c[:, C_LIMIT:C_LIMIT + 8] = 128.0 * np.arange(1, 9)
    return c


class Steps:

    def __init__(self, eng, sem):
        self.eng, self.sem, self.n = eng, sem, 0

    def __call__(self, ins):
        ins.then_inc(self.sem, 1)
        self.n += 1
        self.eng.wait_ge(self.sem, self.n)


def rows_of(t):
    return P if t < LAST else DEC


def attention_units():
    units = []
    for pair in range(PAIRS):
        for a in range(2):
            for i in range(SEQ // P):
                hi = i + 1
                while hi > 0:
                    lo = max(0, hi - 4)
                    units.append((pair, a, i, list(range(lo, hi)), hi == i + 1, lo == 0))
                    hi = lo
        for lo, hi in ((13, 17), (9, 13), (5, 9), (1, 5), (0, 1)):
            units.append((pair, None, LAST, list(range(lo, hi)), hi == 17, lo == 0))
    return units


def stream_step(nc, a):
    (x_prompt, x_sample, cache_k, cache_v, state_ret, c_prompt, c_sample, w_in, w_out, ret_norm_g, sb_norm_g,
     w_ada_mix, b_ada_mix, ln_mix_g, ln_mix_b, w_ada_ffn, b_ada_ffn, ln_ffn_g, ln_ffn_b, w_group, b_group,
     w_router, b_router, w_e_gate, w_e_up, w_e_down, consts, y_prompt, y_sample, k_prompt, v_prompt,
     state_prompt, k_sample, v_sample, state_sample, mod_rows, x1_dram, h2_dram, y_dram) = a

    with ExitStack() as ctx:
        with nc.sbuf_tensor("smalls", [P, SMALLS], F32) as smalls, nc.sbuf_tensor("arena", [P, ARENA - SMALLS], F32) as arena:
            pass
        psum = [ctx.enter_context(nc.psum_tensor(f"psum{i}", [P, 2, 512], F32)) for i in range(4)]

        def bank(i):
            return psum[i // 2][:, i % 2, :]

        def sem(name):
            return ctx.enter_context(nc.semaphore(name))

        top = [0]

        def region(n):
            off = top[0]
            top[0] += n
            return off

        def view(off, *dims, dt=F32):
            n = int(np.prod(dims))
            v = smalls[:, off:off + n] if off < SMALLS else arena[:, off - SMALLS:off - SMALLS + n]
            if dt is not F32:
                v = v.bitcast(dt)
            names = "abcd"[:len(dims)]
            if len(dims) == 1:
                return v
            return v.rearrange(f"p ({' '.join(names)}) -> p {' '.join(names)}",
                               **{k: d for k, d in zip(names, dims)})

        r_const = region(608)
        r_small = region(1552)
        r_tmp = region(2560)
        r_a = region(8704)
        r_w = region(8192)
        r_m = region(9216)
        r_sq = region(4352)
        r_b = region(17920)
        assert top[0] <= ARENA and C_MAIN <= 608, top[0]

        split_places = [("low_odd", r_a, EXPERT_W), ("low_even", r_m, EXPERT_W), ("high", r_b, EXPERT_W),
                        ("h_high", r_b + 12288, KC * P), ("h_low", r_b + 13312, KC * P),
                        ("a_high", r_b + 14336, FC * P), ("a_low", r_b + 14848, FC * P)]

        def named(places, dt):
            named_ctx = ExitStack()
            tensors, at = {}, 0
            for name, off, n in places:
                if off > at:
                    named_ctx.enter_context(nc.sbuf_tensor(f"before_{name}", [P, off - at], F32))
                tensors[name] = named_ctx.enter_context(nc.sbuf_tensor(name, [P, n], dt))
                at = off + n
            named_ctx.close()
            return tensors

        raw = named([("raw_odd", r_a, EXPERT_W), ("raw_even", r_m, EXPERT_W)], F32)
        split = named(split_places, F32R)
        projected_f = named([("hT", r_a, KC * TOK), ("win", r_w, 8192)], F32)
        projected_s = named([("x_low", r_a, KC * TOK), ("win_low", r_w, 8192), ("win_high", r_m, 9 * D),
                             ("x_high", r_b + 8960, KC * TOK)], F32R)
        cst = view(r_const, C_MAIN)
        rot = view(r_sq, C_END - C_MAIN)
        ident = cst[:, C_IDENT:C_IDENT + 128]

        small = [r_small]

        def tiny(*dims, dt=F32):
            off = small[0]
            small[0] += int(np.prod(dims))
            assert small[0] <= r_small + 1552
            return view(off, *dims, dt=dt)

        half_ident = tiny(64).bitcast(BF16)
        half_neg = tiny(64).bitcast(BF16)
        half_negs = tiny(32).bitcast(BF16)
        half_tri = tiny(64).bitcast(BF16)
        half_ones = tiny(64).bitcast(BF16)
        mhalf = tiny(36)
        colv = tiny(72)
        csig = tiny(16)
        silu_c = tiny(8, 2)
        modv = tiny(2, 16)
        rows = tiny(128)
        ones_col = tiny(1)
        stats = tiny(2, 6)
        mv = tiny(9, 2)
        ve = tiny(36)
        rstd = tiny(36)
        nmr = tiny(36)
        rstd_b = tiny(36)
        ln_ve = tiny(18)
        ln_rstd = tiny(18)
        ln_nmr = tiny(18)
        ln_mv = tiny(18, 2)
        sb_sq = tiny(9, 8)
        fin_nm = tiny(9)
        fin_sq = tiny(9)
        sb_rstd = tiny(9, 8)
        ret_stats = tiny(36, 6)
        ret_m = tiny(36)
        ret_d = tiny(36)
        router_w = tiny(8, 20)
        router_b = tiny(20)
        tok_i = tiny(9, dt=I32)

        xt = view(r_m, 9, D)
        mixed = view(r_m, 9, D)
        hT, x_low, x_high = [t[:].rearrange("p (k n) -> p k n", k=KC)
                             for t in (projected_f["hT"], projected_s["x_low"], projected_s["x_high"])]
        mixT = view(r_a, KC, TOK)
        ada_b = [view(r_b + 4096 * i, KC, 512) for i in range(4)]
        ada_m = [view(r_m + 4096 * i, KC, 512) for i in range(2)]
        ada_rows = view(r_sq + C_END - C_MAIN, 2048)
        bias_row = view(r_sq + C_END - C_MAIN, 2, 512)
        row_out = view(r_sq + C_END - C_MAIN + 1024, 2, 512)
        ada_acc = view(r_m + 8192, 2, 512)
        win, win_low = [[t[:, 4096 * i:4096 * i + 4096].rearrange("p (k n) -> p k n", k=KC) for i in range(2)]
                        for t in (projected_f["win"], projected_s["win_low"])]
        win_high = projected_s["win_high"][:].rearrange("p (k n) -> p k n", k=9)[:, 0:KC, 512:1024]
        wout = view(r_w, KC, D)

        qhT = view(r_b, 4, TOK)
        khT = view(r_b + 4352, 4, TOK)
        kh = view(r_b + 8704, 9, 4, 128)
        vr = view(r_b + 13312, 9, 4, 128)
        sqT = view(r_sq, 4, TOK)
        skT = view(r_b, 4, TOK)
        sv = view(r_b + 4352, 9, 512)
        rope_a = view(r_tmp, 4, 128)
        rope_b = view(r_tmp + 512, 4, 128)
        rope_c = view(r_tmp + 1024, 4, 128)
        nat = [view(r_tmp + 1536 + 512 * i, 4, 128) for i in range(2)]
        U = view(r_tmp, 2, 4, 128)
        state_in = view(r_tmp + 1024, 4, 128)
        state_out = view(r_tmp + 1536, 4, 128)
        masked = view(r_tmp + 2048, 2, 128)
        kvs = view(r_tmp + 2304, 2, 128)
        gate_sig = view(r_tmp, 2, 512)
        gate_lin = view(r_tmp + 1024, 2, 512)

        s_rot, s_const, s_rows, s_router = sem("rotations_in"), sem("const_in"), sem("rows_in"), sem("router_in")
        s_xb = [sem(f"x_in{i}") for i in range(3)]
        s_adaB = [sem(f"ada_first_in{i}") for i in range(4)]
        s_adaM = [sem(f"ada_later_in{i}") for i in range(2)]
        s_win = [sem(f"win_in{i}") for i in range(2)]
        s_wout, s_state = sem("wout_in"), sem("state_in")
        s_dv, s_po = sem("dve_steps"), sem("pool_steps")
        s_pH, s_pL = sem("operand_high"), sem("operand_low")
        s_rowT, s_colv, s_csig, s_silu = [sem(n) for n in
            ("rows_turned", "columns_ready", "c_sigmoid", "silu_ready")]
        s_ve, s_rstd, s_xn = sem("variance_ready"), sem("rstd_ready"), sem("x_normed")
        s_adap, s_adae, s_adat, s_mod = [sem(n) for n in
            ("first_ada_ready", "first_ada_copied", "first_ada_turned", "modulation_ready")]
        s_bias = [sem(f"bias_row_in{i}") for i in range(2)]
        s_acc, s_rsum, s_rowo = sem("ada_products"), sem("ada_summed"), sem("mod_row_ready")
        s_modw = [sem(f"mod_row_out{i}") for i in range(2)]
        s_sq = sem("sb_squares")
        s_lt, s_leA, s_leD = sem("x_turned"), sem("hT_by_act"), sem("hT_by_dve")
        s_proj, s_freeA, s_freeD = sem("projected"), sem("projection_read_act"), sem("projection_read_dve")
        s_ra, s_rc, s_rope = sem("rope_parts"), sem("rope_sum"), sem("rope_done")
        s_tr, s_tre = sem("projection_turned"), sem("turned_copied")
        s_ko, s_vo, s_so = [sem(f"k_out{i}") for i in range(2)], sem("v_out"), sem("state_out")
        s_sc, s_kv, s_ro = sem("ret_scores"), sem("ret_kv"), sem("ret_out")
        s_sm, s_kvs, s_U, s_oev = sem("scores_masked"), sem("kv_scaled"), sem("state_updated"), sem("ret_out_copied")
        s_rve, s_rrs, s_gs, s_gm, s_mr = [sem(n) for n in
            ("ret_variance", "ret_rstd", "gate_sigmoid", "gate_ready", "ret_mixed")]
        s_kc = [sem(f"cache_k_in"), sem("cache_v_in")]
        s_qk, s_sig, s_scan, s_wm, s_wt = [sem(n) for n in
            ("scores_ready", "sigmoids_ready", "scan_done", "weights_ready", "weights_turned")]
        s_wte, s_pv, s_ov = [sem(n) for n in
            ("turned_weights_copied", "values_summed", "sb_out_copied")]
        s_kt, s_kte, s_ones = sem("cache_k_turned"), sem("cache_k_copied"), sem("scan_start_ones")
        s_sbv, s_sbr, s_sbn = sem("sb_variance"), sem("sb_rstd"), sem("sb_normed")
        s_mt, s_meA, s_meD = sem("mixed_turned"), sem("mixT_by_act"), sem("mixT_by_dve")
        s_brow, s_x5 = sem("row_tables_in"), [sem(f"x_again_in{i}") for i in range(2)]
        s_op, s_ope, s_ve1, s_nm1, s_ve2, s_nm2 = [sem(n) for n in
            ("out_projected", "out_read", "ln_variance", "ln_shift", "ln0_variance", "ln0_shift")]
        s_xh, s_x1, s_h2a, s_h2 = sem("ln_applied"), sem("x1_ready"), sem("h_scaled"), sem("h2_ready")
        s_x1o, s_h2o = [sem(f"x1_out{i}") for i in range(2)], [sem(f"h2_out{i}") for i in range(2)]
        s_ht, s_hte, s_lg = sem("h2_turned"), sem("h2T_copied"), sem("logits_ready")
        s_rt1, s_rt2, s_asg, s_rank, s_route = [sem(n) for n in
            ("exp_inputs", "exps_ready", "assigned", "ranks_ready", "routed")]
        s_iota, s_oh, s_ids, s_gi = [sem(n) for n in
            ("counts_ready", "one_hots_ready", "lists_summed", "lists_ready")]
        s_e = [[sem(f"expert_{w}_in{i}") for w in ("gate", "up", "down")] for i in range(2)]
        s_edone = sem("expert_done")
        s_idx, s_hg, s_htr, s_hL = sem("index_ready"), sem("rows_gathered"), sem("rows_turned2"), sem("block_h_low")
        s_hH, s_wH, s_wL = sem("block_h_high"), sem("weights_high"), sem("weights_low")
        s_gu, s_sg, s_g1, s_a, s_at, s_aH, s_aL, s_yp, s_ye, s_ys = [sem(n) for n in
            ("gate_up_ready", "gate_sig", "gate_silu", "act_ready", "act_turned", "act_high", "act_low",
             "down_ready", "y_copied", "y_stored")]
        s_frow = sem("final_rows_in")
        s_y0 = [sem(f"y_gathered{i}") for i in range(4)]
        s_x1i = sem("x1_in")
        s_cve, s_crs, s_cnm, s_cxh, s_cg, s_cy = [sem(n) for n in
            ("fin_variance", "fin_first", "fin_shift", "fin_applied", "fin_gained", "fin_ready")]
        s_csq = sem("fin_squares")
        s_cacc, s_yo = sem("fin_sum"), sem("y_out")
        s_go = sem("queue_order")
        s_fill = sem("unused_rows_cleared")

        units = attention_units()
        NU = len(units)
        per_pair = NU // PAIRS
        outs_before = []
        n = 0
        for u in units:
            outs_before.append(n)
            n += u[5]
        N_OUT = n
        ov_after = []
        for u in units:
            if u[5]:
                ov_after.append((ov_after[-1] if ov_after else 0) + (1 if u[2] < LAST else 2))

        col_of = [0, 512, 1024, 2048, 1536, 2560, 3072]
        reader = ["D", "D", "A", "A", "D", "A", "A"]
        steps = []
        for g in range(7):
            if g == 3:
                steps += [(g, pr, ch) for pr in range(4) for ch in range(3)]
            else:
                steps += [(g, t, 0) for t in range(TILES)]
        NS = len(steps)
        assert NS == STEPS_BEFORE[7]
        free_count = []
        cnt = {"A": 0, "D": 0}
        for g, _, _ in steps:
            cnt[reader[g]] += 1
            free_count.append((reader[g], cnt[reader[g]]))
        events = []
        ada_at = {1 + int(1.5 * i): i for i in range(16)}
        ret_within = {}
        turn_no = 0
        split_no = {}

        def split_event(kind, i, c):
            split_no[kind, i, c] = len(split_no)
            events.append(("split", kind, i, c))

        lag = []
        ret_i = 0
        for k, (g, t, ch) in enumerate(steps):
            if k == STEPS_BEFORE[4]:
                for i in range(ret_i, 36 + 1):
                    events.append(("ret", i))
                ret_i = 37
                split_event("x", 0, None)
            for g_next in (4, 5, 6):
                if k == STEPS_BEFORE[g_next] - (g_next > 4):
                    for c in range(KC):
                        split_event("w", g_next, c)
            if g == 4 and t + 1 < TILES:
                split_event("x", t + 1, None)
            if k == STEPS_BEFORE[4]:
                events.append(("retfin",))
            events.append(("proj", k))
            if g in (0, 1, 5):
                lag.append((k, g, t))
            while lag and (k - lag[0][0] >= 2):
                _, g2, t2 = lag.pop(0)
                events.append(("turn", turn_no, g2, t2))
                turn_no += 1
            for name, later in (("adaout", 2), ("adasum", 1), ("ada", 0)):
                if k - later in ada_at:
                    events.append((name, ada_at[k - later]))
            if g == 3 and k > STEPS_BEFORE[3]:
                for _ in range(3):
                    if ret_i <= 36:
                        events.append(("ret", ret_i))
                        if k + 1 < STEPS_BEFORE[4]:
                            ret_within.setdefault(k + 1, []).append(ret_i)
                        ret_i += 1
        N_TURN = turn_no
        assert N_TURN == 27

        def ada_src(j):
            w = w_ada_mix if j < 6 else w_ada_ffn
            return w[0, :, (j % 6) * 512:(j % 6 + 1) * 512].rearrange("(k p) n -> p k n", p=P)

        def ret_pos(i):
            return i // 4, i % 4

        def gamma_chunk(t, h):
            return float(np.exp(LOG_GAMMA[h] * rows_of(t)))

        r_at = r_b + 8960
        om = view(r_at, 3, 512)
        be = view(r_at + 1536, 3, 512)
        wgt = view(r_at + 3072, 3, 512)
        wT = view(r_at + 4608, 3, 4, 128)
        pf = view(r_at + 6144, 3, 514)
        pc = view(r_at + 6144 + 1542, 2, 514)
        sq_junk = view(r_tmp, 64)
        kTs = view(r_a, PAST)
        kc = view(r_a + 2048, 16, 2, 64)
        vc = view(r_a + 4096, 16, 2, 64)
        first_no, cont_no = [], []
        nf = ncn = 0
        for u in units:
            first_no.append(nf)
            cont_no.append(ncn)
            if u[4]:
                nf += 1
            else:
                ncn += 1

        def width(u):
            _, a_, i, tl, _, _ = units[u]
            return sum(64 if (i == LAST and t == 16) else 128 for t in tl)

        def scan_buf(u):
            if units[u][4]:
                return pf[:, first_no[u] % 3, :]
            return pc[:, cont_no[u] % 2, :]

        rows5 = view(r_b, 8, D)
        xin = view(r_b + 8192, 2, D)
        t1 = view(r_b + 8192 + 2048, 2, D)
        x1 = view(r_b + 8192 + 4096, 2, D)
        h2 = view(r_b + 8192 + 6144, 2, D)
        h2T = view(r_b + 8192 + 8192, KC, P)

        def weights(t, off=0):
            return [t[:, off:off + 4096].rearrange("p (k n) -> p k n", k=KC),
                    t[:, off + 4096:off + 8192].rearrange("p (k n) -> p k n", k=KC),
                    t[:, off + 8192:off + 12288].rearrange("p (k n) -> p k n", k=FC)]

        def chunk(w3, c):
            if c < 4:
                return w3[c % 2][:, :, c // 2 * 256:c // 2 * 256 + 256]
            return w3[2][:, 2 * (c - 4):2 * (c - 4) + 2, :]

        raw_w = [weights(raw[n]) for n in ("raw_even", "raw_odd")]
        high_w = weights(split["high"])
        low_w = [weights(split[n]) for n in ("low_even", "low_odd")]
        rows8 = view(r_w + 3584, 4, D)
        sg = view(r_w + 3584 + 4096, 2, 256)
        h_high, h_low = [split[n][:].rearrange("p (k q) -> p k q", k=KC) for n in ("h_high", "h_low")]
        a_high, a_low = [split[n][:].rearrange("p (k q) -> p k q", k=FC) for n in ("a_high", "a_low")]
        h_high_f = split["h_high"][:].bitcast(F32).rearrange("p (a c) -> p a c", a=2)
        a_high_f = split["a_high"][:].bitcast(F32).rearrange("p (k q) -> p k q", k=FC)
        hg = view(r_b + 15360, D)
        yb = view(r_b + 16384, D)
        an = view(r_b + 17408, 2, 256)
        zero_rows = view(r_m + EXPERT_W, D)
        ya = [view(r_b + D * t, D) for t in range(TILES)]
        yc = [view(r_a + D * t, D) for t in range(TILES)]
        x1c = [view(r_m + D * t, D) for t in range(TILES)]

        rt = [r_tmp]

        def rtiny(*dims, dt=F32):
            off = rt[0]
            rt[0] += int(np.prod(dims))
            assert rt[0] <= r_tmp + 2560
            return view(off, *dims, dt=dt)

        lg = rtiny(9, 20)
        gmax = rtiny(9)
        eq = rtiny(9, 4)
        eqm = rtiny(9)
        oh = rtiny(9, 4)
        gsub = rtiny(9, 4)
        gsum = rtiny(9)
        prod = rtiny(9, 16)
        ein = rtiny(9, 4)
        v0 = rtiny(9)
        v1 = rtiny(9)
        a0 = rtiny(9, 4)
        a1 = rtiny(9, 4)
        dd = rtiny(9)
        w0 = rtiny(9)
        w1 = rtiny(9)
        A0 = rtiny(9, 16)
        A1 = rtiny(9, 16)
        Ab = rtiny(72).bitcast(BF16)
        cnt16 = rtiny(16)
        cmp8 = rtiny(16, 8)
        nb = rtiny(16)
        incl = rtiny(16)
        table_f = rtiny(17)
        table = rtiny(17, dt=I32)
        slots = rtiny(9, 16)
        sk_f = rtiny(2, 9)
        slot_i = rtiny(2, 9, dt=I32)
        gi = rtiny(MAX_BLOCKS, dt=I32)
        tok_f = rtiny(9)
        place_oh = view(r_w + 3584, 18, P)
        past = view(r_w + 5888, 18, MAX_BLOCKS + 1)
        block_oh = view(r_w + 6504, 18, MAX_BLOCKS)
        block_tok = view(r_w + 7104, 18, MAX_BLOCKS)
        starts = view(r_w + 7704, MAX_BLOCKS + 1)
        places = view(r_w + 7740, P)
        starts_i = view(r_w + 7868, MAX_BLOCKS + 1, dt=I32)
        places_i = view(r_w + 7904, P, dt=I32)
        slot_block = view(r_w + 8032, 18)
        slot_place = view(r_w + 8052, 18)
        idc = rtiny(1, dt=I32)

        def weights_turned(act, u):
            _, _, i, tl, _, _ = units[u]
            b = bank(3 + u % 2).rearrange("p (t q) -> p t q", q=P)
            act.wait_ge(s_wt, u + 1)
            if u >= 3:
                act.wait_ge(s_pv, u - 2)
            n_full = len(tl) - (i == LAST and tl[-1] == 16)
            last = nc.scalar.activation(wT[:, u % 3, 0:n_full], b[:, 0:n_full], ACT.Copy)
            if n_full < len(tl):
                last = nc.scalar.activation(wT[0:64, u % 3, n_full], b[0:64, n_full], ACT.Copy)
            last.then_inc(s_wte, 1)

        def norm_scalars(step, G, r, col):
            c = slice(col, col + 1)
            step(G.tensor_tensor(ln_rstd[0:r, c], ln_ve[0:r, c], mhalf[0:r, 0:1], ALU.pow))
            step(G.tensor_tensor(ln_nmr[0:r, c], ln_mv[0:r, col, 0:1], ln_rstd[0:r, c], ALU.mult))
            return G.tensor_scalar(ln_nmr[0:r, c], ln_nmr[0:r, c], -1.0, None, ALU.mult)

        block = ctx.enter_context(nc.Block())

        @block.sync
        def _(sp):
            sp.dma_start(cst, consts[:, 0:C_MAIN]).then_inc(s_const, 16)
            for off, src, nr in ((0, c_prompt[0], 8), (8, c_sample[0], 8), (16, b_ada_mix[0], 24),
                                 (40, b_ada_ffn[0], 24), (64, ret_norm_g[0], 4), (68, sb_norm_g[0], 4)):
                sp.dma_start(rows[off:off + nr, :], src.rearrange("(r c) -> r c", r=nr)).then_inc(s_rows, 16)
            sp.dma_start(xt[:, 0:4, :], x_prompt[0, 0:512, :].rearrange("(t p) d -> p t d", p=P)).then_inc(s_xb[0], 16)
            for j in range(2):
                sp.dma_start(ada_b[j], ada_src(j)).then_inc(s_adaB[j], 16)
            sp.dma_start(xt[:, 4:8, :], x_prompt[0, 512:1024, :].rearrange("(t p) d -> p t d", p=P)).then_inc(s_xb[1], 16)
            sp.dma_start(xt[0:DEC, LAST, :], x_sample[0]).then_inc(s_xb[2], 16)
            for j in range(2, 4):
                sp.dma_start(ada_b[j], ada_src(j)).then_inc(s_adaB[j], 16)

            def load_win(g):
                if g >= 2:
                    sp.wait_ge(s_proj, STEPS_BEFORE[g - 1])
                sp.dma_start(win[g % 2], w_in[0, :, col_of[g]:col_of[g] + 512].rearrange("(k p) n -> p k n", p=P)
                             ).then_inc(s_win[g % 2], 16)

            def load_ada(j):
                if j < 6:
                    sp.wait_ge(s_lt, 24)
                    sp.wait_ge(s_adat, 4)
                else:
                    sp.wait_ge(s_acc, 2 * (j - 5))
                sp.dma_start(ada_m[j % 2], ada_src(j)).then_inc(s_adaM[j % 2], 16)
                if j >= 6:
                    sp.wait_ge(s_rowo, 2 * (j - 5))
                b = (b_ada_mix if j < 6 else b_ada_ffn)[0:1, (j % 6) * 512:(j % 6 + 1) * 512]
                sp.dma_start(bias_row[0:1, j % 2], b).then_inc(s_bias[j % 2], 16)

            load_win(0)
            sp.dma_start(rot, consts[:, C_MAIN:C_END]).then_inc(s_rot, 16)
            load_win(1)
            sp.dma_start(router_w[:, :, 0:4], w_group[0].rearrange("(k p) n -> p k n", p=P)).then_inc(s_router, 16)
            sp.dma_start(router_w[:, :, 4:20], w_router[0].rearrange("(k p) n -> p k n", p=P)).then_inc(s_router, 16)
            sp.dma_start(router_b[:, 0:4], b_group[0].unsqueeze(0).to_broadcast([P, 4])).then_inc(s_router, 16)
            sp.dma_start(router_b[:, 4:20], b_router[0].unsqueeze(0).to_broadcast([P, 16])).then_inc(s_router, 16)
            for j in (4, 5, 6, 7):
                load_ada(j)
            load_win(2)
            for j in (8, 9, 10, 11):
                load_ada(j)
            load_win(3)
            sp.wait_ge(s_tre, 18)
            sp.wait_ge(s_rope, 18)
            sp.dma_start(state_in, state_ret[0, 0].rearrange("h k v -> k h v")).then_inc(s_state, 16)
            load_win(4)
            sp.wait_ge(s_U, 36)
            sp.dma_start(state_prompt[0, 0].rearrange("h k v -> k h v"), U[:, 0]).then_inc(s_so, 16)
            sp.dma_start(state_sample[0, 0].rearrange("h k v -> k h v"), state_out).then_inc(s_so, 16)
            load_win(5)
            load_win(6)
            base_a = 21
            for t in range(TILES):
                r = rows_of(t)
                sp.wait_ge(s_freeA, base_a + t + 1)
                dst = k_prompt[0, 0, :, t * P:t * P + r, :] if t < LAST else k_sample[0, 0]
                sp.dma_start(dst.rearrange("h s d -> s h d"),
                             nat[t % 2][0:r].rearrange("p a b -> p (a b)").rearrange("p (h d) -> p h d", h=8)).then_inc(s_ko[t % 2], 16)
            for t in range(TILES):
                r = rows_of(t)
                sp.wait_ge(s_freeA, base_a + 9 + t + 1)
                dst = v_prompt[0, 0, :, t * P:t * P + r, :] if t < LAST else v_sample[0, 0]
                sp.dma_start(dst.rearrange("h s d -> s h d"),
                             sv[0:r, t, :].rearrange("p (h d) -> p h d", h=8)).then_inc(s_vo, 16)
            sp.wait_ge(s_proj, NS)

            def load_cache(pair):
                if pair:
                    sp.wait_ge(s_kt, 4 * pair)
                for hh in range(2):
                    sp.dma_start(kc[:, :, hh, :], cache_k[0, 0, 2 * pair + hh].rearrange("(t p) d -> p t d", p=P)
                                 ).then_inc(s_kc[0], 16)
                if pair:
                    sp.wait_ge(s_pv, per_pair * pair)
                for hh in range(2):
                    sp.dma_start(vc[:, :, hh, :], cache_v[0, 0, 2 * pair + hh].rearrange("(t p) d -> p t d", p=P)
                                 ).then_inc(s_kc[1], 16)

            load_cache(0)
            sp.dma_start(wout, w_out[0].rearrange("(k p) n -> p k n", p=P)).then_inc(s_wout, 16)
            for pair in range(1, PAIRS):
                load_cache(pair)
            sp.wait_ge(s_pv, NU)
            for i in range(2):
                sp.wait_ge(s_modw[i], 16 * 8)
            sp.wait_ge(s_vo, 16 * TILES)

            def mod_row(ada, s, part):
                return mod_rows[ada, s:s + 1, part * D:(part + 1) * D].to_broadcast([P, D])

            for slot, src in enumerate((mod_row(0, 0, 2), mod_row(0, 1, 2), mod_row(1, 0, 1), mod_row(1, 1, 1),
                                        mod_row(1, 0, 0), mod_row(1, 1, 0),
                                        ln_mix_g[0].unsqueeze(0).to_broadcast([P, D]),
                                        ln_mix_b[0].unsqueeze(0).to_broadcast([P, D]))):
                sp.dma_start(rows5[:, slot, :], src).then_inc(s_brow, 16)
            sp.wait_ge(s_ov, N_OUT + PAIRS)

            def load_x(t):
                r = rows_of(t)
                if t >= 2:
                    sp.wait_ge(s_ve1, t - 1)
                src = x_prompt[0, t * P:t * P + r, :] if t < LAST else x_sample[0]
                sp.dma_start(xin[0:r, t % 2, :], src).then_inc(s_x5[t % 2], 16)

            def store_5(t):
                r = rows_of(t)
                sp.wait_ge(s_x1, t + 1)
                sp.dma_start(x1_dram[t * P:t * P + r, :], x1[0:r, t % 2, :]).then_inc(s_x1o[t % 2], 16)
                sp.wait_ge(s_h2, t + 1)
                sp.dma_start(h2_dram[t * P:t * P + r, :], h2[0:r, t % 2, :]).then_inc(s_h2o[t % 2], 16)

            load_x(0)
            load_x(1)

            def load_expert(e, k):
                for i, w in enumerate((w_e_gate, w_e_up, w_e_down)):
                    sp.dma_start(raw_w[k][i], w[0, e].rearrange("(k p) n -> p k n", p=P)).then_inc(s_e[k][i], 16)

            sp.wait_ge(s_mt, 24)
            load_expert(0, 0)
            for t in range(TILES):
                if t + 2 < TILES:
                    load_x(t + 2)
                store_5(t)
            sp.wait_ge(s_op, TILES)
            load_expert(1, 1)
            sp.wait_ge(s_lg, 9)
            sp.wait_ge(s_x1o[0], 16 * 5)
            sp.wait_ge(s_h2o[0], 16 * 5)
            sp.wait_ge(s_x1o[1], 16 * 4)
            sp.wait_ge(s_h2o[1], 16 * 4)
            sp.wait_ge(s_h2, 9)
            sp.wait_ge(s_hg, 16)
            for slot, src in enumerate((mod_row(1, 0, 2), mod_row(1, 1, 2),
                                        ln_ffn_g[0].unsqueeze(0).to_broadcast([P, D]),
                                        ln_ffn_b[0].unsqueeze(0).to_broadcast([P, D]))):
                sp.dma_start(rows8[:, slot, :], src).then_inc(s_frow, 16)
            sp.wait_ge(s_route, 1)
            total = sp.value_load(table[0:1, 16:17], min_val=1, max_val=MAX_BLOCKS - 1)
            with sp.Fori(total, MAX_BLOCKS) as b:
                sp.dma_start(y_dram[bass.ds(b * P, P), :], zero_rows).then_inc(s_fill, 16)
            with sp.Fori(1, EXPERTS // 2) as ee:
                for k in range(2):
                    end = sp.value_load(table[0:1, bass.ds(2 * ee + k - 1, 1)], min_val=1, max_val=MAX_BLOCKS - 1)
                    sp.wait_ge(s_gu, 2 * end)
                    sp.sem_inc(s_go, 1)
                    for i, w in enumerate((w_e_gate, w_e_up, w_e_down)):
                        if i == 2:
                            sp.wait_ge(s_edone, 2 * ee + k - 1)
                        src = w[0, bass.ds(2 * ee + k, 1)].rearrange("e (k p) n -> p (e k) n", p=P)
                        sp.dma_start(raw_w[k][i], src).then_inc(s_e[k][i], 16)
            sp.wait_ge(s_edone, EXPERTS - 1)
            for t in range(TILES):
                r = rows_of(t)
                sp.dma_start(x1c[t][0:r], x1_dram[t * P:t * P + r, :]).then_inc(s_x1i, 16)

            for t in range(TILES):
                r = rows_of(t)
                sp.wait_ge(s_cy, t + 1)
                dst = y_prompt[0, t * P:t * P + r, :] if t < LAST else y_sample[0]
                sp.dma_start(dst, ya[t][0:r]).then_inc(s_yo, 16)
            sp.wait_ge(s_yo, 16 * TILES)
            sp.wait_ge(s_ko[0], 16 * 5)
            sp.wait_ge(s_ko[1], 16 * 4)
            sp.wait_ge(s_so, 32)

        @block.tensor
        def _(pe):
            pe_last = [None]

            def mm(*x, **y):
                pe_last[0] = nc.tensor.matmul(*x, **y)
                return pe_last[0]

            pe.wait_ge(s_const, 16)
            pe.wait_ge(s_rows, 96)
            nc.tensor.transpose(bank(7)[:, 0:72], rows[0:72, :], ident[0:72, 0:72]).then_inc(s_rowT, 1)

            pe.wait_ge(s_silu, 1)
            for j in range(5):
                if j < 4:
                    pe.wait_ge(s_adaB[j], 16)
                    if j >= 2:
                        pe.wait_ge(s_adae, j - 1)
                    for k in range(KC):
                        last = mm(bank(6 + j % 2)[0:2, :], silu_c[:, k, :], ada_b[j][:, k, :],
                                  start=(k == 0), stop=(k == KC - 1))
                    last.then_inc(s_adap, 1)
                if j >= 1:
                    pe.wait_ge(s_adae, j)
                    for e in range(4 * j - 4, 4 * j):
                        last = nc.tensor.transpose(bank(5)[:, 2 * e:2 * e + 2], ada_rows[0:2, e * P:(e + 1) * P],
                                                   ident[0:2, 0:2])
                    last.then_inc(s_adat, 1)
            n = 0
            for b, (t0, t1_) in enumerate(((0, 4), (4, 8), (8, 9))):
                pe.wait_ge(s_xn, t1_)
                for k in range(KC):
                    if n >= 4:
                        pe.wait_ge(s_leA if n % 2 == 0 else s_leD, (n - 4) // 2 + 1)
                    for t in range(t0, t1_):
                        r = rows_of(t)
                        c0 = (t - t0) * P
                        last = nc.tensor.transpose(bank(n % 4)[:, c0:c0 + r], xt[0:r, t, k * P:(k + 1) * P],
                                                   ident[0:r, 0:r])
                    last.then_inc(s_lt, 1)
                    n += 1

            def split_products(out, x_high, x_low, w_high, w_low, start, stop):
                mm(out, x_high, w_high, start=start, stop=False)
                mm(out, x_high, w_low, start=False, stop=False)
                return mm(out, x_low, w_high, start=False, stop=stop)

            def proj(k):
                g, t, ch = steps[k]
                if k == 0:
                    pe.wait_ge(s_leA, 12)
                    pe.wait_ge(s_leD, 12)
                if k == STEPS_BEFORE[g] and g < 4:
                    pe.wait_ge(s_win[g % 2], 16 * (g // 2 + 1))
                if k >= 3:
                    e, c = free_count[k - 3]
                    pe.wait_ge(s_freeA if e == "A" else s_freeD, c)
                w = win[g % 2]
                for c in range(KC):
                    if g == 3:
                        c0, cw = ch * 512, (512 if ch < 2 else DEC)
                        last = mm(bank(k % 3)[:, 0:cw], w[:, c, t * P:(t + 1) * P], hT[:, c, c0:c0 + cw],
                                  start=(c == 0), stop=(c == KC - 1))
                        if c in (1, 4) and len(ret_within.get(k, ())) > c // 4:
                            ret(ret_within[k][c // 4])
                    elif g < 3:
                        r = rows_of(t)
                        last = mm(bank(k % 3)[0:r, :], hT[:, c, t * P:t * P + r], w[:, c, :],
                                  start=(c == 0), stop=(c == KC - 1))
                    else:
                        r = rows_of(t)
                        if k == STEPS_BEFORE[g]:
                            pe.wait_ge(s_pL, split_no["w", g, c] + 1)
                        elif g == 4 and c == 0:
                            pe.wait_ge(s_pL, split_no["x", t, None] + 1)
                        rows = slice(t * P, t * P + r)
                        last = split_products(bank(k % 3)[0:r, :], x_high[:, c, rows], x_low[:, c, rows],
                                              win_high[:, c, :], win_low[g % 2][:, c, :], c == 0, c == KC - 1)
                last.then_inc(s_proj, 1)
                for i in ret_within.get(k, ())[2:]:
                    ret(i)

            def turn(n, g, t):
                r = rows_of(t)
                if n >= 2:
                    pe.wait_ge(s_tre, n - 1)
                if g < 2:
                    pe.wait_ge(s_rope, n + 1)
                    src = nat[n % 2] if g == 0 else kh[:, t]
                else:
                    pe.wait_ge(s_freeA, 21 + t + 1)
                    src = nat[t % 2]
                b = bank(3 if n % 2 == 0 else 7)
                for h in range(4):
                    last = nc.tensor.transpose(b[:, h * P:h * P + r], src[0:r, h, :], ident[0:r, 0:r])
                last.then_inc(s_tr, 1)

            def ret(i):
                if i < 36:
                    t, h = ret_pos(i)
                    r = rows_of(t)
                    if i == 0:
                        pe.wait_ge(s_tre, 18)
                        pe.wait_ge(s_rope, 18)
                        pe.wait_ge(s_freeA, 9)
                        pe.wait_ge(s_rowo, 16)
                    if i >= 1:
                        pe.wait_ge(s_sm, i)
                        pe.wait_ge(s_kvs, i)
                    mm(bank(4)[0:r, 0:r], khT[:, h, t * P:t * P + r], qhT[:, h, t * P:t * P + r],
                       start=True, stop=True).then_inc(s_sc, 1)
                    mm(bank(6)[:, 0:128], kh[0:r, t, h, :], vr[0:r, t, h, :], start=True, stop=True).then_inc(s_kv, 1)
                if i >= 1:
                    j = i - 1
                    t, h = ret_pos(j)
                    r = rows_of(t)
                    pe.wait_ge(s_sm, j + 1)
                    if j >= 1:
                        pe.wait_ge(s_oev, j)
                    o = bank(5)[0:r, 0:128]
                    last = mm(o, masked[0:r, j % 2, 0:r], vr[0:r, t, h, :], start=True, stop=(t == 0))
                    if t == LAST:
                        pe.wait_ge(s_state, 16)
                        last = mm(o, qhT[:, h, t * P:t * P + r], state_in[:, h, :], start=False, stop=True)
                    elif t > 0:
                        pe.wait_ge(s_U, (t - 1) * 4 + h + 1)
                        last = mm(o, qhT[:, h, t * P:t * P + r], U[:, t % 2, h, :], start=False, stop=True)
                    last.then_inc(s_ro, 1)

            for ev in events:
                if ev[0] == "proj":
                    proj(ev[1])
                elif ev[0] == "turn":
                    turn(*ev[1:])
                elif ev[0] == "adasum":
                    i = ev[1]
                    pe.wait_ge(s_acc, i + 1)
                    if i >= 2:
                        pe.wait_ge(s_rowo, i - 1)
                    mm(bank(5 + i % 2)[0:1, :], ones_col, ada_acc[:, i % 2], start=True, stop=True).then_inc(s_rsum, 1)
                elif ev[0] == "ret" and not any(ev[1] in inside for inside in ret_within.values()):
                    ret(ev[1])
            for n in (25, 26):
                pe.wait_ge(s_tre, n + 1)
            pe.wait_ge(s_freeA, 39)

            def cache_turn(n):
                pair, q = n // 4, n % 4
                pe.wait_ge(s_kc[0], 32 * (pair + 1))
                if n:
                    pe.wait_ge(s_kte, n)
                for j in range(4):
                    last = nc.tensor.transpose(bank(7)[:, j * P:(j + 1) * P],
                                               kc[:, 4 * q + j].rearrange("p h d -> p (h d)"), ident)
                last.then_inc(s_kt, 1)

            def qk(u):
                pair, a_, i, tl, first, _ = units[u]
                if u >= 3:
                    pe.wait_ge(s_sig, 2 * (u - 2))
                z = bank(u % 3)
                w = width(u)
                if i < LAST:
                    mm(z[:, 0:w], sqT[64 * a_:64 * a_ + 64, pair, i * P:(i + 1) * P],
                       skT[64 * a_:64 * a_ + 64, pair, tl[0] * P:tl[0] * P + w], start=True, stop=not first)
                    if first:
                        last = mm(z[:, w - P:w], half_ident, half_neg, start=False, stop=True)
                else:
                    for hh in range(2):
                        q = sqT[64 * hh:64 * hh + 64, pair, SEQ:SEQ + DEC]
                        zz = z[64 * hh:64 * hh + 64]
                        if first:
                            pe.wait_ge(s_kte, 4 * pair + 4)
                            mm(zz[:, 0:w - DEC], q, kTs[64 * hh:64 * hh + 64, tl[0] * P:PAST], start=True, stop=True)
                            mm(zz[:, w - DEC:w], q, skT[64 * hh:64 * hh + 64, pair, SEQ:SEQ + DEC],
                               start=False, stop=False, skip_group_check=True)
                        else:
                            mm(zz[:, 0:w], q, kTs[64 * hh:64 * hh + 64, tl[0] * P:tl[0] * P + w],
                               start=True, stop=True)
                    if first:
                        mm(z[:, w - DEC:w], half_ident, half_negs, start=False, stop=True, skip_group_check=True)
                pe_last[0].then_inc(s_qk, 1)

            def wturn(u):
                _, _, i, tl, _, _ = units[u]
                pe.wait_ge(s_wm, u + 1)
                if u >= 2:
                    pe.wait_ge(s_wte, u - 1)
                for j, t in enumerate(tl):
                    r = 64 if (i == LAST and t == 16) else P
                    last = nc.tensor.transpose(bank(3 + u % 2)[0:r, j * P:(j + 1) * P],
                                               wgt[:, u % 3, j * P:j * P + r], ident)
                last.then_inc(s_wt, 1)

            def pv(u):
                pair, a_, i, tl, first, lastu = units[u]
                o = outs_before[u]
                pe.wait_ge(s_wte, u + 1)
                if first and o >= 2:
                    pe.wait_ge(s_ov, ov_after[o - 2])
                ob = bank(5 + o % 2)
                for j, t in enumerate(tl):
                    st, sp_ = (first and j == 0), (lastu and j == len(tl) - 1)
                    if i < LAST:
                        last = mm(ob[:, 0:64], wT[:, u % 3, j, :], sv[:, t, (2 * pair + a_) * 64:(2 * pair + a_) * 64 + 64],
                                  start=st, stop=sp_)
                    elif t == 16:
                        last = mm(ob[:, 0:128], wT[0:64, u % 3, j, :], sv[0:64, LAST, pair * P:(pair + 1) * P],
                                  start=st, stop=sp_)
                    else:
                        if first and j == 0:
                            pe.wait_ge(s_kc[1], 32 * (pair + 1))
                        last = mm(ob[:, 0:128], wT[:, u % 3, j, :], vc[:, t].rearrange("p h d -> p (h d)"),
                                  start=st, stop=sp_)
                last.then_inc(s_pv, 1)

            for u in range(NU + 4):
                if u < NU:
                    lu = u % per_pair
                    if lu in (8, 12, 16, 20):
                        cache_turn(4 * (u // per_pair) + lu // 4 - 2)
                    qk(u)
                if 2 <= u < NU + 2:
                    wturn(u - 2)
                if u >= 4:
                    pv(u - 4)

            n = 0
            pe.wait_ge(s_wte, NU)
            pe.wait_ge(s_kte, 16)
            for half in range(2):
                for b, (t0, t1_) in enumerate(((0, 4), (4, 8), (8, 9))):
                    for k in range(4 * half, 4 * half + 4):
                        if half:
                            pe.wait_ge(s_sbn, t1_)
                        if n >= 4:
                            pe.wait_ge(s_meA if n - 4 < 12 else s_meD, (n - 4) % 12 + 1)
                        for t in range(t0, t1_):
                            r = rows_of(t)
                            c0 = (t - t0) * P
                            last = nc.tensor.transpose(bank(n % 4)[:, c0:c0 + r], mixed[0:r, t, k * P:(k + 1) * P],
                                                       ident[0:r, 0:r])
                        last.then_inc(s_mt, 1)
                        n += 1
            pe.wait_ge(s_ov, N_OUT + PAIRS)
            pe.wait_ge(s_meA, 12)
            pe.wait_ge(s_meD, 12)
            pe.wait_ge(s_wout, 16)

            def h2_turned(t):
                r = rows_of(t)
                pe.wait_ge(s_h2, t + 1)
                if t:
                    pe.wait_ge(s_hte, t)
                for k in range(KC):
                    last = nc.tensor.transpose(psum[2][:, k // 4, (k % 4) * P:(k % 4) * P + r],
                                               h2[0:r, t % 2, k * P:(k + 1) * P], ident[0:r, 0:r])
                last.then_inc(s_ht, 1)

            def logits(t):
                r = rows_of(t)
                pe.wait_ge(s_hte, t + 1)
                if t == 0:
                    pe.wait_ge(s_router, 64)
                for k in range(KC):
                    last = mm(bank(6)[0:r, t * 20:t * 20 + 20], h2T[:, k, 0:r], router_w[:, k, :],
                              start=(k == 0), stop=(k == KC - 1))
                last.then_inc(s_lg, 1)

            for t in range(TILES):
                r = rows_of(t)
                if t >= 2:
                    pe.wait_ge(s_ope, t - 1)
                for hh in range(2):
                    for k in range(KC):
                        last = mm(psum[t % 2][0:r, hh, :], mixT[:, k, t * P:t * P + r],
                                  wout[:, k, hh * 512:(hh + 1) * 512], start=(k == 0), stop=(k == KC - 1))
                    if hh == 1:
                        last.then_inc(s_op, 1)
                    elif t >= 3:
                        logits(t - 3)
                if t >= 2:
                    h2_turned(t - 2)
            logits(LAST - 2)
            for t in (LAST - 1, LAST):
                h2_turned(t)
                logits(t)
            pe.wait_ge(s_asg, 1)
            pe.wait_ge(s_ope, TILES)
            mm(bank(0)[:, 0:144], half_tri, Ab, start=True, stop=False)
            for n in range(1, 9):
                mm(bank(0)[:, 16 * n:144], half_ones, Ab[:, 0:144 - 16 * n], start=False, stop=(n == 8))
            for n in range(9):
                last = mm(bank(1)[:, 0:16], half_ones, Ab[:, 16 * n:16 * n + 16], start=(n == 0), stop=(n == 8))
            last.then_inc(s_rank, 1)

            for n in range(18):
                if n % 9 == 0:
                    pe.wait_ge(s_oh, n // 9 + 1)
                r = rows_of(n % 9)
                last = mm(bank(2)[:, 0:MAX_BLOCKS], place_oh[0:r, n, :], block_tok[0:r, n, :], start=(n == 0), stop=(n == 17))
            last.then_inc(s_ids, 1)

            def block_turn(b):
                pe.wait_ge(s_hg, 16 * (b + 1))
                for k in range(KC):
                    last = nc.tensor.transpose(psum[1][:, k // 4, (k % 4) * P:(k % 4 + 1) * P],
                                               hg[:, k * P:(k + 1) * P], ident)
                last.then_inc(s_htr, 1)

            pe.wait_ge(s_route, 1)
            block_turn(0)
            with pe.Fori(0, EXPERTS // 2) as ee:
                for k in range(2):
                    first = pe.value_load(table[0:1, bass.ds(2 * ee + k, 1)], min_val=0, max_val=MAX_BLOCKS - 1)
                    end = pe.value_load(table[0:1, bass.ds(2 * ee + k + 1, 1)], min_val=1, max_val=MAX_BLOCKS - 1)
                    with pe.Fori(first, end) as b:
                        pe.wait_ge(s_hL, b + 1)
                        for half in range(2):
                            pe.wait_ge(s_wL, 12 * ee + 6 * k + 2 * half + 2)
                            for w in range(2):
                                cols = slice(half * 256, half * 256 + 256)
                                for c in range(KC):
                                    last = split_products(bank(half)[:, w * 256:w * 256 + 256], h_high[:, c, :],
                                                          h_low[:, c, :], high_w[w][:, c, cols], low_w[k][w][:, c, cols],
                                                          c == 0, c == KC - 1)
                            last.then_inc(s_gu, 1)
                        for half in range(2):
                            pe.wait_ge(s_a, 2 * b + half + 1)
                            for f in range(2):
                                last = nc.tensor.transpose(bank(6 + half)[:, f * P:(f + 1) * P],
                                                           an[:, half, f * P:(f + 1) * P], ident)
                            last.then_inc(s_at, 1)
                            if half == 0:
                                pe.wait_ge(s_hg, 16 * b + 32)
                                for c in range(KC):
                                    last = nc.tensor.transpose(psum[1][:, c // 4, (c % 4) * P:(c % 4 + 1) * P],
                                                               hg[:, c * P:(c + 1) * P], ident)
                                last.then_inc(s_htr, 1)
                        pe.wait_ge(s_ye, b + 1)
                        pe.wait_ge(s_wL, 12 * ee + 6 * k + 6)
                        for f in range(FC):
                            if f % 2 == 0:
                                pe.wait_ge(s_aL, 2 * b + f // 2 + 1)
                            for hh in range(2):
                                cols = slice(hh * 512, hh * 512 + 512)
                                last = split_products(psum[2][:, hh, :], a_high[:, f, :], a_low[:, f, :],
                                                      high_w[2][:, f, cols], low_w[k][2][:, f, cols], f == 0, f == FC - 1)
                        last.then_inc(s_yp, 1)
                    nc.tensor.transpose(bank(7)[0:64, 0:64], ident[0:64, 0:64], ident[0:64, 0:64]).then_inc(s_edone, 1)

        @block.scalar
        def _(act):
            A = nc.scalar.activation
            act.wait_ge(s_colv, 1)
            A(csig, colv[:, 0:16], ACT.Sigmoid).then_inc(s_csig, 1)
            for j in range(4):
                act.wait_ge(s_adap, j + 1)
                A(ada_rows[0:2, j * 512:(j + 1) * 512], bank(6 + j % 2)[0:2, :], ACT.Copy).then_inc(s_adae, 1)
            act.wait_ge(s_mod, 1)
            n = 0
            for b, wd in enumerate((512, 512, DEC)):
                s = int(b == 2)
                for k in range(KC):
                    if n % 2 == 0:
                        act.wait_ge(s_lt, n + 1)
                        A(hT[:, k, b * 512:b * 512 + wd], bank(n % 4)[:, 0:wd], ACT.Identity,
                          bias=modv[:, s, k:k + 1], scale=modv[:, s, 8 + k:9 + k]).then_inc(s_leA, 1)
                    n += 1

            def turned(n, g, t):
                r = rows_of(t)
                dst = (qhT, khT, None, None, None, skT)[g]
                act.wait_ge(s_tr, n + 1)
                b = bank(3 if n % 2 == 0 else 7)
                A(dst[:, :, t * P:t * P + r], b.rearrange("p (h c) -> p h c", h=4)[:, :, 0:r], ACT.Copy).then_inc(s_tre, 1)

            for ev in events:
                if ev[0] == "proj":
                    k = ev[1]
                    g, t, ch = steps[k]
                    if g in (2, 3, 5, 6):
                        act.wait_ge(s_proj, k + 1)
                    r = rows_of(t)
                    b = bank(k % 3)
                    if g == 2:
                        A(vr[0:r, t].rearrange("p h d -> p (h d)"), b[0:r], ACT.Copy).then_inc(s_freeA, 1)
                    elif g == 3:
                        cw = 512 if ch < 2 else DEC
                        if (t, ch) == (0, 0):
                            act.wait_ge(s_rowo, 16)
                            for m in s_modw:
                                act.wait_ge(m, 128)
                        A(sqT[:, t, ch * 512:ch * 512 + cw], b[:, 0:cw], ACT.Copy).then_inc(s_freeA, 1)
                    elif g == 4:
                        act.wait_ge(s_proj, k + 1)
                        if t == 0:
                            act.wait_ge(s_so, 32)
                        if t >= 2:
                            act.wait_ge(s_gm, t - 1)
                        A(gate_sig[0:r, t % 2], b[0:r], ACT.Sigmoid).then_inc(s_gs, 1)
                    elif g == 5:
                        if t == 0:
                            act.wait_ge(s_mr, 9)
                        if t >= 2:
                            act.wait_ge(s_ko[t % 2], 16 * (t // 2))
                            act.wait_ge(s_tr, 18 + t - 1)
                        A(nat[t % 2][0:r].rearrange("p h d -> p (h d)"), b[0:r], ACT.Copy).then_inc(s_freeA, 1)
                    elif g == 6:
                        A(sv[0:r, t], b[0:r], ACT.Copy).then_inc(s_freeA, 1)
                elif ev[0] == "split":
                    _, kind, i, c = ev
                    if kind == "x":
                        act.wait_ge(s_ro, 36)
                        rows = slice(i * P, i * P + rows_of(i))
                        A(x_high[:, :, rows], hT[:, :, rows], ACT.Copy).then_inc(s_pH, 1)
                    else:
                        if c == 0:
                            act.wait_ge(s_win[i % 2], 16 * (i // 2 + 1))
                            act.wait_ge(s_proj, STEPS_BEFORE[i])
                        A(win_high[:, c, :], win[i % 2][:, c, :], ACT.Copy).then_inc(s_pH, 1)
                elif ev[0] == "turn":
                    turned(*ev[1:])
                elif ev[0] == "adaout":
                    i = ev[1]
                    j, st = 4 + i // 2, i % 2
                    act.wait_ge(s_rowo, i + 1)
                    act.dma_start(mod_rows[j // 6, st:st + 1, (j % 6) * 512:(j % 6 + 1) * 512],
                                  row_out[0:1, i % 2]).then_inc(s_modw[i % 2], 16)
                elif ev[0] == "ret":
                    i = ev[1]
                    if i < 36:
                        t, h = ret_pos(i)
                        act.wait_ge(s_kv, i + 1)
                        if i >= 2:
                            act.wait_ge(s_U, i - 1)
                        if i == 0:
                            act.wait_ge(s_rope, 18)
                            act.wait_ge(s_tr, 18)
                        A(kvs[:, i % 2], bank(6)[:, 0:128], ACT.Copy, scale=gamma_chunk(t, h)).then_inc(s_kvs, 1)
                    if i >= 1:
                        j = i - 1
                        t, h = ret_pos(j)
                        r = rows_of(t)
                        act.wait_ge(s_ro, j + 1)
                        if j == 0:
                            act.wait_ge(s_rowo, 16)
                        A(mixed[0:r, t, h * P:(h + 1) * P], bank(5)[0:r, 0:128], ACT.Copy).then_inc(s_oev, 1)

            def squares(v):
                pair, a_, i, _, _, _ = units[v]
                o = outs_before[v]
                act.wait_ge(s_ov, ov_after[o])
                r = rows_of(i)
                for hh in ((a_,) if i < LAST else (0, 1)):
                    h = 2 * pair + hh
                    if s_sq_n[0]:
                        act.wait_ge(s_sq, s_sq_n[0])
                    s_sq_n[0] += 1
                    A(sq_junk[0:r], mixed[0:r, i, 512 + h * 64:512 + h * 64 + 64], ACT.Square,
                      accum_out=sb_sq[0:r, i, h:h + 1]).then_inc(s_sq, 1)

            s_sq_n = [0]
            for u in range(NU + 5):
                lu = u % per_pair
                if u < NU:
                    if lu in (8, 12, 16, 20):
                        n = 4 * (u // per_pair) + lu // 4 - 2
                        act.wait_ge(s_kt, n + 1)
                        A(kTs[:, (n % 4) * 512:(n % 4 + 1) * 512], bank(7), ACT.Copy).then_inc(s_kte, 1)
                    w = width(u)
                    act.wait_ge(s_qk, u + 1)
                    if u >= 3:
                        act.wait_ge(s_scan, u - 2)
                    A(om[:, u % 3, 0:w], bank(u % 3)[:, 0:w], ACT.Sigmoid, scale=-CHUNK_SCALE).then_inc(s_sig, 1)
                    if u >= 3:
                        act.wait_ge(s_wm, u - 2)
                    A(be[:, u % 3, 0:w], bank(u % 3)[:, 0:w], ACT.Sigmoid, scale=CHUNK_SCALE).then_inc(s_sig, 1)
                if 2 <= u < NU + 2:
                    weights_turned(act, u - 2)
                if u >= 5 and units[u - 5][5]:
                    squares(u - 5)

            n = 0
            for b, wd in enumerate((512, 512, DEC)):
                for k in range(4):
                    act.wait_ge(s_mt, n + 1)
                    A(mixT[:, k, b * 512:b * 512 + wd], bank(n % 4)[:, 0:wd], ACT.Copy,
                      scale=colv[:, 64 + k:65 + k]).then_inc(s_meA, 1)
                    n += 1
            for t in range(TILES + 2):
                v = t - 1
                if 0 <= v < TILES:
                    r = rows_of(v)
                    act.wait_ge(s_nm2, v + 1)
                    if v >= 2:
                        act.wait_ge(s_h2o[v % 2], 16 * (v // 2))
                        act.wait_ge(s_ht, v - 1)
                    A(h2[0:r, v % 2], x1[0:r, v % 2], ACT.Identity, bias=ln_nmr[0:r, 9 + v:10 + v],
                      scale=ln_rstd[0:r, 9 + v:10 + v]).then_inc(s_h2a, 1)
                v = t - 2
                if v >= 0:
                    r = rows_of(v)
                    act.wait_ge(s_ht, v + 1)
                    if v:
                        act.wait_ge(s_lg, v)
                    A(h2T[:, :, 0:r], psum[2].rearrange("p a (c q) -> p (a c) q", q=P)[:, :, 0:r], ACT.Copy).then_inc(s_hte, 1)
                if t < TILES:
                    r = rows_of(t)
                    act.wait_ge(s_nm1, t + 1)
                    A(t1[0:r, t % 2], t1[0:r, t % 2], ACT.Identity, bias=ln_nmr[0:r, t:t + 1],
                      scale=ln_rstd[0:r, t:t + 1]).then_inc(s_xh, 1)
            act.wait_ge(s_rt1, 1)
            A(gsub, gsub, ACT.Exp).then_inc(s_rt2, 1)
            act.wait_ge(s_rt1, 2)
            A(dd, dd, ACT.Exp).then_inc(s_rt2, 1)

            def high_parts(k, cs, loads=None):
                for c in cs:
                    if loads is not None and c in (0, 1, 4):
                        act.wait_ge(s_e[k][min(c, 2)], loads)
                    A(chunk(high_w, c), chunk(raw_w[k], c), ACT.Copy).then_inc(s_wH, 1)

            act.wait_ge(s_h2, TILES)
            high_parts(0, range(6), 16)
            act.wait_ge(s_route, 1)
            act.wait_ge(s_h2o[0], 80)
            act.wait_ge(s_h2o[1], 64)
            act.wait_ge(s_htr, 1)
            A(h_high.rearrange("p (a c) q -> p a (c q)", a=2), psum[1][:], ACT.Copy).then_inc(s_hH, 1)
            act.sem_inc(s_ye, 1)
            act.sem_inc(s_ys, 16)

            def act_pair(ee, final):
                for k in range(2):
                    nxt, loads = 1 - k, 16 * ee + 16 + 16 * k
                    follows = not (final and k == 1)
                    first = act.value_load(table[0:1, bass.ds(2 * ee + k, 1)], min_val=0, max_val=MAX_BLOCKS - 1)
                    end = act.value_load(table[0:1, bass.ds(2 * ee + k + 1, 1)], min_val=1, max_val=MAX_BLOCKS - 1)
                    with act.Fori(first, end) as b:
                        act.wait_ge(s_gu, 2 * b + 1)
                        A(sg[:, 0], bank(0)[:, 0:256], ACT.Sigmoid).then_inc(s_sg, 1)
                        if follows:
                            with act.If(b + 1 == end):
                                high_parts(nxt, (0,), loads)
                        act.wait_ge(s_gu, 2 * b + 2)
                        A(sg[:, 1], bank(1)[:, 0:256], ACT.Sigmoid).then_inc(s_sg, 1)
                        for half in range(2):
                            act.wait_ge(s_at, 2 * b + half + 1)
                            A(a_high[:, 2 * half:2 * half + 2], bank(6 + half)[:, 0:256].rearrange(
                                "p (f q) -> p f q", f=2), ACT.Copy).then_inc(s_aH, 1)
                        act.wait_ge(s_htr, b + 2)
                        A(h_high.rearrange("p (a c) q -> p a (c q)", a=2), psum[1][:], ACT.Copy).then_inc(s_hH, 1)
                        if follows:
                            with act.If(b + 1 == end):
                                high_parts(nxt, (1, 2, 3), loads)
                        act.wait_ge(s_yp, b + 1)
                        act.wait_ge(s_ys, 16 * b + 16)
                        A(yb.rearrange("p (a c) -> p a c", a=2), psum[2][:], ACT.Copy).then_inc(s_ye, 1)
                        act.wait_ge(s_ye, b + 2)
                        act.dma_start(y_dram[bass.ds(b * P, P), :], yb).then_inc(s_ys, 16)
                    if follows:
                        high_parts(nxt, (4, 5), loads)

            with act.Fori(0, EXPERTS // 2 - 1) as ee:
                act_pair(ee, False)
            act_pair(EXPERTS // 2 - 1, True)

            for t in range(TILES + 3):
                if t < TILES:
                    r = rows_of(t)
                    act.wait_ge(s_y0[t % 4], 32 * (t // 4 + 1))
                    A(ya[t][0:r], ya[t][0:r], ACT.Copy, scale=w0[0:r, t:t + 1]).then_inc(s_crs, 1)
                v = t - 1
                if 0 <= v < TILES:
                    r = rows_of(v)
                    act.wait_ge(s_cve, v + 1)
                    A(yc[v][0:r], ya[v][0:r], ACT.Square, bias=fin_nm[0:r, v:v + 1],
                      accum_out=fin_sq[0:r, v:v + 1]).then_inc(s_csq, 1)
                v = t - 3
                if v >= 0:
                    r = rows_of(v)
                    act.wait_ge(s_cnm, v + 1)
                    A(ya[v][0:r], ya[v][0:r], ACT.Identity, bias=ln_nmr[0:r, v:v + 1],
                      scale=ln_rstd[0:r, v:v + 1]).then_inc(s_cxh, 1)

        @block.vector
        def _(dve):
            V = nc.vector
            step = Steps(dve, s_dv)
            TT, TS, STT = V.tensor_tensor, V.tensor_scalar, V.scalar_tensor_tensor

            def done(ins, s, value):
                ins.then_inc(s, 1)
                dve.wait_ge(s, value)

            step(V.memset(mhalf, -0.5))
            step(V.memset(half_ones, 1.0))
            step(V.memset(ones_col, 1.0))
            step(V.memset(ret_stats, 0.0))
            dve.wait_ge(s_const, 16)
            step(V.tensor_copy(half_ident, ident))
            step(V.tensor_copy(half_neg, cst[:, C_NEG:C_NEG + 128]))
            step(V.tensor_copy(half_negs, cst[:, C_NEGS:C_NEGS + 64]))
            step(V.tensor_copy(half_tri, cst[:, C_TRI:C_TRI + 128]))
            dve.wait_ge(s_rowT, 1)
            done(V.tensor_copy(colv, bank(7)[:, 0:72]), s_colv, 1)

            def variance(src, r, dst):
                for hh in range(2):
                    step(V.bn_stats(stats[0:r, hh, :], src[:, hh * 512:(hh + 1) * 512]))
                step(V.bn_aggr(dst, stats[0:r].rearrange("p a b -> p (a b)")))

            def batch_ln(b, t0, t1_):
                dve.wait_ge(s_xb[b], 16)
                for t in range(t0, t1_):
                    variance(xt[0:rows_of(t), t, :], rows_of(t), mv[0:rows_of(t), t, :])
                r = rows_of(t0)
                done(TS(ve[0:r, t0:t1_], mv[0:r, t0:t1_, 1], EPS, None, ALU.add), s_ve, b + 1)
                dve.wait_ge(s_rstd, b + 1)
                step(STT(nmr[0:r, t0:t1_], mv[0:r, t0:t1_, 0], -1.0, rstd[0:r, t0:t1_], ALU.mult, ALU.mult))
                for t in range(t0, t1_):
                    x = xt[0:r, t, :]
                    done(TS(x, x, rstd[0:r, t:t + 1], nmr[0:r, t:t + 1], ALU.mult, ALU.add), s_xn, t + 1)

            dve.wait_ge(s_csig, 1)
            TT(silu_c.rearrange("p k s -> p s k"), colv[:, 0:16].rearrange("p (s k) -> p s k", s=2),
               csig.rearrange("p (s k) -> p s k", s=2), ALU.mult).then_inc(s_silu, 1)
            batch_ln(0, 0, 4)
            batch_ln(1, 4, 8)
            batch_ln(2, 8, 9)

            dve.wait_ge(s_adat, 4)
            step(TT(modv, bank(5)[:, 0:32].rearrange("p (e s) -> p s e", s=2),
                    colv[:, 16:32].unsqueeze(1).to_broadcast([P, 2, 16]), ALU.add))
            done(TS(modv[:, :, 8:16], modv[:, :, 8:16], 1.0, None, ALU.add), s_mod, 1)
            n = 0
            for b, wd in enumerate((512, 512, DEC)):
                s = int(b == 2)
                for k in range(KC):
                    if n % 2 == 1:
                        dve.wait_ge(s_lt, n + 1)
                        TS(hT[:, k, b * 512:b * 512 + wd], bank(n % 4)[:, 0:wd], modv[:, s, 8 + k:9 + k],
                           modv[:, s, k:k + 1], ALU.mult, ALU.add).then_inc(s_leD, 1)
                    n += 1

            def ret(i):
                t, h = ret_pos(i)
                r = rows_of(t)
                dve.wait_ge(s_sc, i + 1)
                if i == 0:
                    dve.wait_ge(s_rope, 18)
                    dve.wait_ge(s_tr, 18)
                if i >= 2:
                    dve.wait_ge(s_ro, i - 1)
                TT(masked[0:r, i % 2, 0:r], bank(4)[0:r, 0:r], cst[0:r, C_CAUSAL:C_CAUSAL + r], ALU.mult).then_inc(s_sm, 1)
                dve.wait_ge(s_kvs, i + 1)
                if t == 0:
                    done(V.tensor_copy(U[:, 1, h, :], kvs[:, i % 2]), s_U, i + 1)
                elif t == LAST:
                    dve.wait_ge(s_state, 16)
                    done(STT(state_out[:, h, :], state_in[:, h, :], gamma_chunk(t, h), kvs[:, i % 2], ALU.mult, ALU.add),
                         s_U, i + 1)
                else:
                    dve.wait_ge(s_ro, (t - 1) * 4 + h + 1)
                    done(STT(U[:, (t + 1) % 2, h, :], U[:, t % 2, h, :], gamma_chunk(t, h), kvs[:, i % 2],
                             ALU.mult, ALU.add), s_U, i + 1)

            def head_stats(i):
                t, h = ret_pos(i)
                dve.wait_ge(s_oev, i + 1)
                r = rows_of(t)
                V.bn_stats(ret_stats[0:r, i, :], mixed[0:r, t, h * P:(h + 1) * P]).then_inc(s_dv, 1)
                step.n += 1

            for ev in events:
                if ev[0] == "proj":
                    k = ev[1]
                    g, t, ch = steps[k]
                    r = rows_of(t)
                    b = bank(k % 3)[0:r].rearrange("p (h d) -> p h d", h=4)
                    if g < 2:
                        n = free_count[k][1]
                        dve.wait_ge(s_rot, 16)
                        dve.wait_ge(s_proj, k + 1)
                        if n > 1:
                            dve.wait_ge(s_rc, n - 1)
                        b4 = b.rearrange("p h (a d) -> p h a d", a=2)
                        cos = rot[0:r, 64 * t:64 * t + 64].unsqueeze(1).unsqueeze(1).to_broadcast([r, 4, 2, 64])
                        sin = rot[0:r, 64 * TILES + 128 * t:64 * TILES + 128 * t + 128].rearrange("p (a d) -> p a d", a=2)\
                            .unsqueeze(1).to_broadcast([r, 4, 2, 64])
                        TT(rope_a[0:r].rearrange("p h (a d) -> p h a d", a=2), b4, cos, ALU.mult).then_inc(s_ra, 1)
                        done(TT(rope_b[0:r].rearrange("p h (a d) -> p h a d", a=2), b4[:, :, ::-1, :], sin, ALU.mult),
                             s_freeD, n)
                        dve.wait_ge(s_ra, n)
                    elif g == 4:
                        n = free_count[k][1]
                        dve.wait_ge(s_gs, t + 1)
                        if t >= 2:
                            dve.wait_ge(s_mr, t - 1)
                        done(TT(gate_lin[0:r, t % 2], gate_sig[0:r, t % 2], bank(k % 3)[0:r], ALU.mult), s_freeD, n)
                        m4 = mixed[0:r, t, 0:512].rearrange("p (h d) -> p h d", h=4)
                        step(TT(m4, m4, rstd_b[0:r, 4 * t:4 * t + 4].unsqueeze(2).to_broadcast([r, 4, 128]), ALU.mult))
                        done(TT(m4, m4, ret_m[0:r, 4 * t:4 * t + 4].unsqueeze(2).to_broadcast([r, 4, 128]), ALU.add),
                             s_gm, t + 1)
                elif ev[0] == "split":
                    _, kind, i, c = ev
                    dve.wait_ge(s_pH, split_no[ev[1:]] + 1)
                    if kind == "x":
                        if i == 0:
                            dve.wait_ge(s_proj, STEPS_BEFORE[4])
                        rows = slice(i * P, i * P + rows_of(i))
                        TT(x_low[:, :, rows], hT[:, :, rows], x_high[:, :, rows].bitcast(F32), ALU.subtract).then_inc(s_pL, 1)
                    else:
                        TT(win_low[i % 2][:, c, :], win[i % 2][:, c, :], win_high[:, c, :].bitcast(F32),
                           ALU.subtract).then_inc(s_pL, 1)
                elif ev[0] == "adaout":
                    i = ev[1]
                    j = 4 + i // 2
                    dve.wait_ge(s_rsum, i + 1)
                    dve.wait_ge(s_bias[j % 2], 16 * ((j - 4) // 2 + 1))
                    if i >= 2:
                        dve.wait_ge(s_modw[i % 2], 16 * (i // 2))
                    done(STT(row_out[0:1, i % 2], bank(5 + i % 2)[0:1, :], 1.0 if j in (8, 9) else 0.0,
                             bias_row[0:1, j % 2], ALU.add, ALU.add), s_rowo, i + 1)
                elif ev[0] == "ada":
                    i = ev[1]
                    j, st = 4 + i // 2, i % 2
                    dve.wait_ge(s_adaM[j % 2], 16 * ((j - 4) // 2 + 1))
                    if i >= 2:
                        dve.wait_ge(s_rsum, i - 1)
                    w, o = ada_m[j % 2], ada_acc[:, i % 2]
                    step(TS(o, w[:, 0], silu_c[:, 0, st:st + 1], None, ALU.mult))
                    for k in range(1, KC - 1):
                        step(STT(o, w[:, k], silu_c[:, k, st:st + 1], o, ALU.mult, ALU.add))
                    done(STT(o, w[:, KC - 1], silu_c[:, KC - 1, st:st + 1], o, ALU.mult, ALU.add), s_acc, i + 1)
                elif ev[0] == "ret":
                    if ev[1] < 36:
                        ret(ev[1])
                    if ev[1] >= 2:
                        head_stats(ev[1] - 2)
                elif ev[0] == "retfin":
                    head_stats(35)
                    dve.wait_ge(s_dv, step.n)
                    step(TT(ret_m, ret_stats[:, :, 1], ret_stats[:, :, 4], ALU.add))
                    step(TT(ret_d, ret_stats[:, :, 1], ret_stats[:, :, 4], ALU.subtract))
                    step(TT(ve, ret_stats[:, :, 2], ret_stats[:, :, 5], ALU.add))
                    step(TS(ve, ve, 1.0 / 128, EPS, ALU.mult, ALU.add))
                    step(STT(ret_d, ret_d, 0.25, ret_d, ALU.mult, ALU.mult))
                    done(TT(ve, ve, ret_d, ALU.add), s_rve, 1)
                    dve.wait_ge(s_rrs, 1)
                    step(STT(ret_m, ret_m, -0.5, rstd_b, ALU.mult, ALU.mult))

            dve.wait_ge(s_mr, 9)
            dve.wait_ge(s_ro, 36)
            dve.wait_ge(s_proj, NS)
            step(V.memset(sb_sq, 1.0))
            done(V.memset(pf[:, :, 512:513], 1.0), s_ones, 1)
            for u in range(NU + 4):
                if u < NU:
                    w = width(u)
                    pb = scan_buf(u)
                    o = om[:, u % 3, 0:w]
                    dve.wait_ge(s_sig, 2 * u + 1)
                    if not units[u][4]:
                        prev = scan_buf(u - 1)
                        pw = 512 - width(u - 1)
                        step(V.tensor_copy(pb[:, 512:513], prev[:, pw:pw + 1]))
                        init = pb[:, 512:513]
                    else:
                        init = 1.0
                    lo = 512 - w
                    pbr = pb[:, 511:lo - 1:-1] if lo > 0 else pb[:, 511::-1]
                    done(V.tensor_tensor_scan(pbr, om[:, u % 3, w - 1::-1], om[:, u % 3, w - 1::-1], init,
                                              ALU.mult, ALU.min), s_scan, u + 1)
                    dve.wait_ge(s_sig, 2 * u + 2)
                    if u >= 3:
                        dve.wait_ge(s_wt, u - 2)
                    done(TT(wgt[:, u % 3, 0:w], be[:, u % 3, 0:w], pb[:, lo + 1:513], ALU.mult), s_wm, u + 1)
                if u == 3 * per_pair + 10:
                    dve.wait_ge(s_sq, (N_OUT + PAIRS) // 4 * 3)
                    done(TS(sb_sq[:, :, 0:6], sb_sq[:, :, 0:6], 1.0 / 64, EPS, ALU.mult, ALU.add), s_sbv, 1)
                if u >= 4 and units[u - 4][5]:
                    v = u - 4
                    pair, a_, i, _, _, _ = units[v]
                    ob = bank(5 + outs_before[v] % 2)
                    dve.wait_ge(s_pv, v + 1)
                    if i < LAST:
                        V.tensor_copy(mixed[:, i, 512 + (2 * pair + a_) * 64:512 + (2 * pair + a_) * 64 + 64],
                                      ob[:, 0:64]).then_inc(s_ov, 1)
                    else:
                        for hh in range(2):
                            V.tensor_copy(mixed[0:64, LAST, 512 + (2 * pair + hh) * 64:512 + (2 * pair + hh) * 64 + 64],
                                          ob[64 * hh:64 * hh + 64, 64 * hh:64 * hh + 64]).then_inc(s_ov, 1)
            dve.wait_ge(s_ov, N_OUT + PAIRS)
            dve.wait_ge(s_sq, N_OUT + PAIRS)
            done(TS(sb_sq[:, :, 6:8], sb_sq[:, :, 6:8], 1.0 / 64, EPS, ALU.mult, ALU.add), s_sbv, 2)
            dve.wait_ge(s_sbr, 2)
            for t in range(TILES):
                r = rows_of(t)
                m83 = mixed[0:r, t, 512:1024].rearrange("p (h d) -> p h d", h=8)
                TT(m83, m83, sb_rstd[0:r, t].unsqueeze(2).to_broadcast([r, 8, 64]), ALU.mult).then_inc(s_sbn, 1)
            n = 12
            for b, wd in enumerate((512, 512, DEC)):
                for k in range(4, KC):
                    dve.wait_ge(s_mt, n + 1)
                    TS(mixT[:, k, b * 512:b * 512 + wd], bank(n % 4)[:, 0:wd], colv[:, 64 + k:65 + k], None,
                       ALU.mult).then_inc(s_meD, 1)
                    n += 1

            def variance_out(x, r, col, s, value):
                variance(x, r, ln_mv[0:r, col, :])
                done(TS(ln_ve[0:r, col:col + 1], ln_mv[0:r, col, 1:2], EPS, None, ALU.add), s, value)

            dve.wait_ge(s_brow, 128)
            for t in range(TILES + 1):
                v = t - 1
                if v >= 0:
                    r = rows_of(v)
                    x = t1[0:r, v % 2]
                    dve.wait_ge(s_xh, v + 1)
                    step(TT(x, x, rows5[0:r, 6], ALU.mult))
                    if v >= 2:
                        dve.wait_ge(s_x1o[v % 2], 16 * (v // 2))
                        dve.wait_ge(s_h2a, v - 1)
                    done(TT(x1[0:r, v % 2], x, rows5[0:r, 7], ALU.add), s_x1, v + 1)
                    variance_out(x1[0:r, v % 2], r, 9 + v, s_ve2, v + 1)
                if t < TILES:
                    r = rows_of(t)
                    s = int(t == LAST)
                    x = t1[0:r, t % 2]
                    dve.wait_ge(s_op, t + 1)
                    done(TT(x, psum[t % 2][0:r].rearrange("p a b -> p (a b)"), rows5[0:r, s], ALU.mult), s_ope, t + 1)
                    dve.wait_ge(s_x5[t % 2], 16 * (t // 2 + 1))
                    step(STT(x, xin[0:r, t % 2], ALPHA, x, ALU.mult, ALU.add))
                    variance_out(x, r, t, s_ve1, t + 1)
            r = rows_of(LAST)
            dve.wait_ge(s_h2a, TILES)
            step(TT(h2[0:r, LAST % 2], h2[0:r, LAST % 2], rows5[0:r, 3], ALU.mult))
            dve.wait_ge(s_h2, LAST)
            done(TT(h2[0:r, LAST % 2], h2[0:r, LAST % 2], rows5[0:r, 5], ALU.add), s_h2, TILES)

            step(V.memset(zero_rows, 0.0))
            step(V.memset(lg, 0.0))
            dve.wait_ge(s_lg, 9)
            step(TT(lg[:, 0:8], bank(6)[:, 0:160].rearrange("p (t n) -> p t n", t=8),
                    router_b.unsqueeze(1).to_broadcast([P, 8, 20]), ALU.add))
            step(TT(lg[0:DEC, 8], bank(6)[0:DEC, 160:180], router_b[0:DEC], ALU.add))
            firsts = cst[:, C_FIRST:C_FIRST + 4].unsqueeze(1).to_broadcast([P, 9, 4])

            def wide(v, n_=4):
                return v.unsqueeze(2).to_broadcast([P, 9, n_])

            def first_max(src, mx, dst):
                step(V.tensor_reduce(mx, src, AX.X, ALU.max))
                step(TT(eq, src, wide(mx), ALU.is_equal))
                step(TT(eq, eq, firsts, ALU.mult))
                step(V.tensor_reduce(eqm, eq, AX.X, ALU.max))
                step(TT(dst, eq, wide(eqm), ALU.is_equal))

            g4 = lg[:, :, 0:4]
            first_max(g4, gmax, oh)
            done(TT(gsub, g4, wide(gmax), ALU.subtract), s_rt1, 1)
            step(TT(oh, oh, wide(cst[:, C_VALID:C_VALID + 9]), ALU.mult))
            p4 = prod.rearrange("p t (g j) -> p t g j", g=4)
            for g in range(4):
                step(TT(p4[:, :, g, :], lg[:, :, 4 + 4 * g:8 + 4 * g], oh[:, :, g:g + 1].to_broadcast([P, 9, 4]), ALU.mult))
            step(V.tensor_reduce(ein, p4.rearrange("p t g j -> p t j g"), AX.X, ALU.add))
            first_max(ein, v0, a0)
            step(STT(ein, a0, NEG, ein, ALU.mult, ALU.add))
            first_max(ein, v1, a1)
            dve.wait_ge(s_rt2, 1)
            done(TT(dd, v1, v0, ALU.subtract), s_rt1, 2)
            for A_, a_ in ((A0, a0), (A1, a1)):
                for g in range(4):
                    step(TT(A_.rearrange("p t (g j) -> p t g j", g=4)[:, :, g, :], a_,
                            oh[:, :, g:g + 1].to_broadcast([P, 9, 4]), ALU.mult))
            done(TT(Ab.rearrange("p (t e) -> p t e", t=9), A0, A1, ALU.add), s_asg, 1)
            step(V.tensor_reduce(gsum, gsub, AX.X, ALU.add))
            dve.wait_ge(s_rt2, 2)
            step(TS(w1, dd, 1.0, None, ALU.add))
            step(TT(gsum, gsum, w1, ALU.mult))
            step(V.reciprocal(w0, gsum))
            step(TT(w1, w0, dd, ALU.mult))
            dve.wait_ge(s_rank, 1)
            step(V.tensor_copy(cnt16, bank(1)[:, 0:16]))
            step(TT(cmp8, cnt16.unsqueeze(2).to_broadcast([P, 16, 8]),
                    cst[:, C_LIMIT:C_LIMIT + 8].unsqueeze(1).to_broadcast([P, 16, 8]), ALU.is_gt))
            step(V.tensor_reduce(nb, cmp8, AX.X, ALU.add))
            step(TS(nb, nb, 1.0, None, ALU.add))
            step(V.tensor_tensor_scan(incl, nb, nb, 0.0, ALU.add, ALU.max))
            step(V.memset(table_f, 0.0))
            step(V.tensor_copy(table_f[:, 1:17], incl))
            step(V.tensor_copy(table, table_f))
            step(TS(cnt16, table_f[:, 0:16], 128.0, None, ALU.mult))
            step(TT(slots, bank(0)[:, 0:144].rearrange("p (t e) -> p t e", t=9),
                    cnt16.unsqueeze(1).to_broadcast([P, 9, 16]), ALU.add))
            for kk, A_ in enumerate((A0, A1)):
                step(TT(A_, A_, slots, ALU.mult))
                step(V.tensor_reduce(sk_f[:, kk], A_, AX.X, ALU.add))
            slot = sk_f.rearrange("p a t -> p (a t)")
            dve.wait_ge(s_iota, 3)
            step(TT(past, slot.unsqueeze(2).to_broadcast([P, 18, MAX_BLOCKS + 1]),
                    starts.unsqueeze(1).to_broadcast([P, 18, MAX_BLOCKS + 1]), ALU.is_ge))
            step(TT(block_oh, past[:, :, 0:MAX_BLOCKS], past[:, :, 1:MAX_BLOCKS + 1], ALU.subtract))
            step(V.tensor_reduce(slot_block, past[:, :, 1:MAX_BLOCKS + 1], AX.X, ALU.add))
            step(STT(slot_place, slot_block, -128.0, slot, ALU.mult, ALU.add))
            for kk in range(2):
                step(TT(block_tok[:, 9 * kk:9 * kk + 9], block_oh[:, 9 * kk:9 * kk + 9],
                        tok_f.unsqueeze(2).to_broadcast([P, 9, MAX_BLOCKS]), ALU.mult))
            for kk in range(2):
                done(TT(place_oh[:, 9 * kk:9 * kk + 9], slot_place[:, 9 * kk:9 * kk + 9].unsqueeze(2).to_broadcast([P, 9, P]),
                        places.unsqueeze(1).to_broadcast([P, 9, P]), ALU.is_equal), s_oh, kk + 1)
            done(V.tensor_copy(slot_i, sk_f), s_route, 1)
            dve.wait_ge(s_ids, 1)
            done(V.tensor_copy(gi, bank(2)[:, 0:MAX_BLOCKS]), s_gi, 1)
            def low_parts(k, cs, before):
                for c in cs:
                    dve.wait_ge(s_wH, before + c + 1)
                    TT(chunk(low_w[k], c), chunk(raw_w[k], c), chunk(high_w, c).bitcast(F32), ALU.subtract).then_inc(s_wL, 1)

            h_low_2 = h_low.rearrange("p (a c) q -> p a (c q)", a=2)
            low_parts(0, (0, 1, 2), 0)
            dve.wait_ge(s_hH, 1)
            TT(h_low_2, psum[1][:], h_high_f, ALU.subtract).then_inc(s_hL, 1)
            low_parts(0, (3, 4, 5), 0)

            def dve_pair(ee, final):
                for k in range(2):
                    nxt, before = 1 - k, 12 * ee + 6 * k + 6
                    follows = not (final and k == 1)
                    first = dve.value_load(table[0:1, bass.ds(2 * ee + k, 1)], min_val=0, max_val=MAX_BLOCKS - 1)
                    end = dve.value_load(table[0:1, bass.ds(2 * ee + k + 1, 1)], min_val=1, max_val=MAX_BLOCKS - 1)
                    with dve.Fori(first, end) as b:
                        for half in range(2):
                            dve.wait_ge(s_sg, 2 * b + half + 1)
                            TT(an[:, half], sg[:, half], bank(half)[:, 0:256], ALU.mult).then_inc(s_g1, 1)
                            dve.wait_ge(s_g1, 2 * b + half + 1)
                            TT(an[:, half], an[:, half], bank(half)[:, 256:512], ALU.mult).then_inc(s_a, 1)
                            if follows and half == 0:
                                with dve.If(b + 1 == end):
                                    low_parts(nxt, (0,), before)
                        for half in range(2):
                            dve.wait_ge(s_aH, 2 * b + half + 1)
                            TT(a_low[:, 2 * half:2 * half + 2], bank(6 + half)[:, 0:256].rearrange(
                                "p (f q) -> p f q", f=2), a_high_f[:, 2 * half:2 * half + 2], ALU.subtract).then_inc(s_aL, 1)
                        dve.wait_ge(s_hH, b + 2)
                        TT(h_low_2, psum[1][:], h_high_f, ALU.subtract).then_inc(s_hL, 1)
                        if follows:
                            with dve.If(b + 1 == end):
                                low_parts(nxt, (1, 2, 3), before)
                    if follows:
                        low_parts(nxt, (4, 5), before)

            with dve.Fori(0, EXPERTS // 2 - 1) as ee:
                dve_pair(ee, False)
            dve_pair(EXPERTS // 2 - 1, True)

            dve.wait_ge(s_frow, 64)
            dve.wait_ge(s_x1i, 16 * TILES)
            for t in range(TILES + 3):
                if t < TILES:
                    r = rows_of(t)
                    x = ya[t][0:r]
                    dve.wait_ge(s_crs, t + 1)
                    step(STT(x, yc[t][0:r], w1[0:r, t:t + 1], x, ALU.mult, ALU.add))
                    step(TT(x, x, rows8[0:r, int(t == LAST)], ALU.mult))
                    done(STT(x, x1c[t][0:r], ALPHA, x, ALU.mult, ALU.add, accum_out=fin_nm[0:r, t:t + 1]), s_cacc, t + 1)
                    done(TS(fin_nm[0:r, t:t + 1], fin_nm[0:r, t:t + 1], -1.0 / D, None, ALU.mult), s_cve, t + 1)
                v = t - 3
                if v >= 0:
                    r = rows_of(v)
                    dve.wait_ge(s_cxh, v + 1)
                    TT(ya[v][0:r], ya[v][0:r], rows8[0:r, 2], ALU.mult).then_inc(s_cg, 1)

        @block.gpsimd
        def _(pool):
            G = nc.gpsimd
            step = Steps(pool, s_po)
            step(G.iota(tok_i, [[P, 9]], base=0, channel_multiplier=1))
            for b, (t0, t1_) in enumerate(((0, 4), (4, 8), (8, 9))):
                r = rows_of(t0)
                pool.wait_ge(s_ve, b + 1)
                G.tensor_tensor(rstd[0:r, t0:t1_], ve[0:r, t0:t1_], mhalf[0:r, t0:t1_], ALU.pow).then_inc(s_rstd, 1)
            n = 0
            for ev in events:
                if ev[0] == "proj":
                    g, t, _ = steps[ev[1]]
                    r = rows_of(t)
                    if g < 2:
                        n += 1
                        pool.wait_ge(s_freeD, n)
                        pool.wait_ge(s_ra, n)
                        G.tensor_tensor(rope_c[0:r], rope_a[0:r], rope_b[0:r], ALU.add).then_inc(s_rc, 1)
                        pool.wait_ge(s_rc, n)
                        if g == 0 and t >= 2:
                            pool.wait_ge(s_tr, t - 1)
                        c = (C_GQ, C_GK)[g]
                        dst = nat[t % 2] if g == 0 else kh[:, t]
                        G.tensor_tensor(dst[0:r], rope_c[0:r], cst[0:r, c:c + 4].unsqueeze(2).to_broadcast([r, 4, 128]),
                                        ALU.mult).then_inc(s_rope, 1)
                        pool.wait_ge(s_rope, n)
                    elif g == 4:
                        pool.wait_ge(s_gm, t + 1)
                        m = mixed[0:r, t, 0:512]
                        G.tensor_tensor(m, m, gate_lin[0:r, t % 2], ALU.mult).then_inc(s_mr, 1)
                elif ev[0] == "retfin":
                    pool.wait_ge(s_rve, 1)
                    G.tensor_tensor(rstd_b, ve, mhalf, ALU.pow).then_inc(s_rrs, 1)
            for i, heads in enumerate((slice(0, 6), slice(6, 8))):
                pool.wait_ge(s_sbv, i + 1)
                n_ = heads.stop - heads.start
                G.tensor_tensor(sb_rstd[:, :, heads], sb_sq[:, :, heads],
                                mhalf[:, 0:1].unsqueeze(2).to_broadcast([P, 9, n_]), ALU.pow).then_inc(s_sbr, 1)
            for t in range(TILES + 1):
                v = t - 1
                if v >= 0:
                    r = rows_of(v)
                    s = int(v == LAST)
                    pool.wait_ge(s_ve2, v + 1)
                    norm_scalars(step, G, r, 9 + v).then_inc(s_nm2, 1)
                    if v < LAST:
                        pool.wait_ge(s_h2a, v + 1)
                        h = h2[0:r, v % 2]
                        step(G.tensor_tensor(h, h, rows5[0:r, 2 + s], ALU.mult))
                        G.tensor_tensor(h, h, rows5[0:r, 4 + s], ALU.add).then_inc(s_h2, 1)
                if t < TILES:
                    pool.wait_ge(s_ve1, t + 1)
                    norm_scalars(step, G, rows_of(t), t).then_inc(s_nm1, 1)
            pool.wait_ge(s_h2, TILES)
            pool.wait_ge(s_op, TILES)
            G.iota(starts_i, [[P, MAX_BLOCKS + 1]], base=0, channel_multiplier=0).then_inc(s_po, 1)
            G.iota(places_i, [[1, P]], base=0, channel_multiplier=0).then_inc(s_po, 1)
            step.n += 2
            pool.wait_ge(s_po, step.n)
            G.tensor_copy(starts, starts_i).then_inc(s_iota, 1)
            G.tensor_copy(places, places_i).then_inc(s_iota, 1)
            G.tensor_copy(tok_f, tok_i).then_inc(s_iota, 1)
            pool.wait_ge(s_route, 1)
            pool.wait_ge(s_gi, 1)
            pool.wait_ge(s_h2o[0], 80)
            pool.wait_ge(s_h2o[1], 64)
            total = pool.value_load(table[0:1, 16:17], min_val=1, max_val=MAX_BLOCKS - 1)
            G.tensor_copy(idc, gi[:, 0:1]).then_inc(s_idx, 1)
            pool.wait_ge(s_idx, 1)
            pool.indirect_dma_start(hg, None, h2_dram, bass.IndirectOffsetOnAxis(ap=idc[:, 0:1], axis=0)).then_inc(s_hg, 16)
            with pool.Fori(1, total + 1) as b:
                pool.wait_ge(s_htr, b)
                pool.wait_ge(s_hg, 16 * b)
                pool.sem_inc(s_fill, 16)
                G.tensor_copy(idc, gi[:, bass.ds(b, 1)]).then_inc(s_idx, 1)
                pool.wait_ge(s_idx, b + 1)
                pool.sem_inc(s_go, 1)
                pool.indirect_dma_start(hg, None, h2_dram, bass.IndirectOffsetOnAxis(ap=idc[:, 0:1], axis=0)).then_inc(s_hg, 16)
            pool.wait_ge(s_fill, 16 * MAX_BLOCKS)
            pool.wait_ge(s_ys, 16 * total + 16)
            pool.sem_inc(s_go, 1)
            pool.wait_ge(s_edone, EXPERTS)
            pool.sem_inc(s_go, 1)

            def gather(t):
                r = rows_of(t)
                for kk, dst in enumerate((ya[t], yc[t])):
                    pool.indirect_dma_start(dst[0:r], None, y_dram,
                                            bass.IndirectOffsetOnAxis(ap=slot_i[0:r, kk, t:t + 1], axis=0)).then_inc(s_y0[t % 4], 16)

            for t in range(3):
                gather(t)
            pool.wait_ge(s_frow, 64)
            for t in range(TILES + 3):
                if t + 3 < TILES:
                    if t:
                        pool.wait_ge(s_csq, t)
                    gather(t + 3)
                v = t - 1
                if 0 <= v < TILES:
                    r, c = rows_of(v), slice(v, v + 1)
                    pool.wait_ge(s_csq, v + 1)
                    step(G.tensor_scalar(fin_sq[0:r, c], fin_sq[0:r, c], 1.0 / D, EPS, ALU.mult, ALU.add))
                    step(G.tensor_tensor(ln_rstd[0:r, c], fin_sq[0:r, c], mhalf[0:r, 0:1], ALU.pow))
                    G.tensor_tensor(ln_nmr[0:r, c], fin_nm[0:r, c], ln_rstd[0:r, c], ALU.mult).then_inc(s_cnm, 1)
                v = t - 3
                if v >= 0:
                    r = rows_of(v)
                    pool.wait_ge(s_cg, v + 1)
                    G.tensor_tensor(ya[v][0:r], ya[v][0:r], rows8[0:r, 3], ALU.add).then_inc(s_cy, 1)


def launch_shapes():
    return [("y_prompt", (1, SEQ, D)), ("y_sample", (1, DEC, D)), ("k_prompt", (1, 1, SB_HEADS, SEQ, HD)),
            ("v_prompt", (1, 1, SB_HEADS, SEQ, HD)), ("state_prompt", (1, 1, RET_HEADS, 128, 128)),
            ("k_sample", (1, 1, SB_HEADS, DEC, HD)), ("v_sample", (1, 1, SB_HEADS, DEC, HD)),
            ("state_sample", (1, 1, RET_HEADS, 128, 128))]


_INS = ['x_prompt', 'x_sample', 'cache_sb_k', 'cache_sb_v', 'state_ret', 'c_prompt', 'c_sample', 'w_in', 'w_out',
        'ret_norm_g', 'sb_norm_g', 'w_ada_mix', 'b_ada_mix', 'ln_mix_g', 'ln_mix_b', 'w_ada_ffn', 'b_ada_ffn',
        'ln_ffn_g', 'ln_ffn_b', 'w_group', 'b_group', 'w_router', 'b_router', 'w_e_gate', 'w_e_up', 'w_e_down']


def kernel(**inputs):
    import concourse.bacc as _bacc
    from concourse.bass_utils import run_bass_kernel_spmd as _run

    nc = _bacc.Bacc("TRN2", target_bir_lowering=False, num_devices=1)
    arrays, args = {}, []
    for name in _INS:
        arr = np.ascontiguousarray(inputs[name])
        arrays[f"in_{name}"] = arr
        args.append(nc.dram_tensor(f"in_{name}", arr.shape, mybir.dt.from_np(arr.dtype), kind="ExternalInput").ap())
    arrays["in_consts"] = shape_constants()
    args.append(nc.dram_tensor("in_consts", (P, C_END), F32, kind="ExternalInput").ap())
    for name, shape in launch_shapes():
        args.append(nc.dram_tensor(f"out_{name}", shape, F32, kind="ExternalOutput").ap())
    for name, shape, dt in (("mod_rows", (2, 2, 3 * D), F32), ("x1_rows", (TOK, D), F32), ("h2_rows", (TOK, D), F32),
                            ("expert_rows", (MAX_BLOCKS * P, D), F32)):
        args.append(nc.dram_tensor(name, shape, dt, kind="Internal").ap())
    stream_step(nc, args)
    r = _run(nc, [arrays], core_ids=[0])
    return tuple(r.results[0][f"out_{name}"] for name, _ in launch_shapes())
```
